# Optimizing a Trainium2 kernel written in Bass

```python
import jax, jax.numpy as jnp
from jax import lax
import numpy as np

D_MODEL = 1024
BATCH = 1
SEQ = 256
DEPTH = 1

CHUNK = 64
Q_BLOCK = 128
EPS = 1e-6
MLA_HEADS = 8
QK_NOPE = 64
QK_ROPE = 32
QK_HEAD = QK_NOPE + QK_ROPE
V_HEAD = 64
Q_LORA = 256
KV_LORA = 128
ROPE_THETA = 10000.0
LRU_WIDTH = 1024
LRU_BLOCKS = 8
LRU_BW = LRU_WIDTH // LRU_BLOCKS
CONV_WIDTH = 4
LRU_C = 8.0
PEER_HEADS = 8
N_KEYS = 128
N_EXPERTS = N_KEYS * N_KEYS
PEER_DKEY = 256
PEER_HALF = PEER_DKEY // 2
PEER_TOPK = 16
TOKEN_BLOCK = 128
IN_COLS = Q_LORA + KV_LORA + QK_ROPE + 2 * LRU_WIDTH + 2 * D_MODEL
IN_SPLITS = [Q_LORA, Q_LORA + KV_LORA, Q_LORA + KV_LORA + QK_ROPE,
             Q_LORA + KV_LORA + QK_ROPE + LRU_WIDTH,
             Q_LORA + KV_LORA + QK_ROPE + 2 * LRU_WIDTH]


def rms_norm(x, g):
    xf = x.astype(jnp.float32)
    y = xf * lax.rsqrt(jnp.mean(xf * xf, axis=-1, keepdims=True) + EPS)
    return (y * g.astype(jnp.float32)).astype(x.dtype)

def apply_rope(t, cos, sin):
    t1, t2 = jnp.split(t, 2, axis=-1)
    return jnp.concatenate([t1 * cos - t2 * sin, t1 * sin + t2 * cos], axis=-1)

def mla_attention(c_q, c_kv, k_rope, positions, q_a_norm_g, w_uq, kv_a_norm_g, w_ukv,
                  q_norm_g, k_norm_g):
    B, S, _ = c_q.shape
    H = MLA_HEADS
    q = (rms_norm(c_q, q_a_norm_g) @ w_uq).reshape(B, S, H, QK_HEAD)
    kv = (rms_norm(c_kv, kv_a_norm_g) @ w_ukv).reshape(B, S, H, QK_NOPE + V_HEAD)
    k_nope, v = kv[..., :QK_NOPE], kv[..., QK_NOPE:]
    k = jnp.concatenate([k_nope, jnp.broadcast_to(k_rope[:, :, None, :], (B, S, H, QK_ROPE))], axis=-1)
    q = rms_norm(q, q_norm_g)
    k = rms_norm(k, k_norm_g)
    inv_freq = 1.0 / (ROPE_THETA ** (jnp.arange(0, QK_ROPE, 2, dtype=jnp.float32) / QK_ROPE))
    ang = positions.astype(jnp.float32)[..., None] * inv_freq
    cos = jnp.cos(ang)[:, :, None, :].astype(q.dtype)
    sin = jnp.sin(ang)[:, :, None, :].astype(q.dtype)
    q = jnp.concatenate([q[..., :QK_NOPE], apply_rope(q[..., QK_NOPE:], cos, sin)], axis=-1)
    k = jnp.concatenate([k[..., :QK_NOPE], apply_rope(k[..., QK_NOPE:], cos, sin)], axis=-1)
    nb = S // Q_BLOCK
    qb = q.reshape(B, nb, Q_BLOCK, H, QK_HEAD).transpose(1, 0, 2, 3, 4)
    key_chunk = jnp.arange(S) // CHUNK
    scale = QK_HEAD ** -0.5
    neg = jnp.finfo(jnp.float32).min

    def block(args):
        qi, bi = args
        s = jnp.einsum('bqhd,bkhd->bhqk', qi, k, preferred_element_type=jnp.float32) * scale
        q_chunk = (bi * Q_BLOCK + jnp.arange(Q_BLOCK)) // CHUNK
        mask = key_chunk[None, :] <= q_chunk[:, None]
        p = jax.nn.softmax(jnp.where(mask, s, neg), axis=-1).astype(v.dtype)
        return jnp.einsum('bhqk,bkhd->bqhd', p, v)

    o = lax.map(block, (qb, jnp.arange(nb)))
    return o.transpose(1, 0, 2, 3, 4).reshape(B, S, H * V_HEAD)

def rg_lru_branch(xb, gb, conv_w, conv_b, w_rg, b_rg, w_ig, b_ig, lru_lambda):
    B, S, C = xb.shape
    xc = lax.conv_general_dilated(xb, conv_w[:, None, :], window_strides=(1,),
                                  padding=[(CONV_WIDTH - 1, 0)],
                                  dimension_numbers=('NWC', 'WIO', 'NWC'),
                                  feature_group_count=C) + conv_b
    xblk = xc.reshape(B, S, LRU_BLOCKS, LRU_BW)
    r = jax.nn.sigmoid(jnp.einsum('bsni,nio->bsno', xblk, w_rg).reshape(B, S, C) + b_rg)
    i = jax.nn.sigmoid(jnp.einsum('bsni,nio->bsno', xblk, w_ig).reshape(B, S, C) + b_ig)
    log_a = (-LRU_C * r.astype(jnp.float32)) * jax.nn.softplus(-lru_lambda.astype(jnp.float32))
    a = jnp.exp(log_a)
    b = jnp.sqrt(-jnp.expm1(2.0 * log_a)) * (i * xc).astype(jnp.float32)

    def combine(e1, e2):
        a1, b1 = e1
        a2, b2 = e2
        return a1 * a2, a2 * b1 + b2

    _, h = lax.associative_scan(combine, (a, b), axis=1)
    return h.astype(xb.dtype) * jax.nn.gelu(gb)

def peer_ffn(h, w_query, sub_keys, expert_u, expert_v):
    B, S, D = h.shape
    hb = h.reshape((B * S) // TOKEN_BLOCK, TOKEN_BLOCK, D)
    K = PEER_TOPK

    def block(xt):
        q = (xt @ w_query).reshape(TOKEN_BLOCK, PEER_HEADS, 2, PEER_HALF)
        s = jnp.einsum('thpd,hpnd->thpn', q, sub_keys, preferred_element_type=jnp.float32)
        s_top, i_top = lax.top_k(s, K)
        cand = (s_top[:, :, 0, :, None] + s_top[:, :, 1, None, :]).reshape(TOKEN_BLOCK, PEER_HEADS, K * K)
        cand_idx = (i_top[:, :, 0, :, None] * N_KEYS + i_top[:, :, 1, None, :]).reshape(TOKEN_BLOCK, PEER_HEADS, K * K)
        best, pos = lax.top_k(cand, K)
        idx = jnp.take_along_axis(cand_idx, pos, axis=-1)
        g = jax.nn.softmax(best, axis=-1)
        u = expert_u[idx]
        v = expert_v[idx]
        act = jax.nn.gelu(jnp.einsum('td,thkd->thk', xt, u))
        return jnp.einsum('thk,thkd->td', (g * act).astype(xt.dtype), v)

    return lax.map(block, hb).reshape(B, S, D)

def _normal(key, shape, scale):
    return jax.random.normal(key, shape, jnp.float32) * scale

def first_inputs(seed: int = 0) -> dict:
    key = jax.random.key(seed)
    ks = jax.random.split(key, 32)
    L, D, H = DEPTH, D_MODEL, MLA_HEADS
    x = _normal(ks[0], (BATCH, SEQ, D), 1.0)
    c = _normal(ks[1], (BATCH, D), 1.0)
    positions = (jax.random.randint(ks[2], (BATCH, 1), 0, 4096, dtype=jnp.int32)
                 + jnp.arange(SEQ, dtype=jnp.int32)[None, :]).astype(jnp.int32)
    u = jax.random.uniform(ks[21], (L, LRU_WIDTH), jnp.float32, 0.9, 0.999)
    a_base = u ** (1.0 / LRU_C)
    lru_lambda = jnp.log(a_base) - jnp.log1p(-a_base)
    return {
        'x': x,
        'c': c,
        'positions': positions,
        'w_ada': _normal(ks[3], (L, D, 6 * D), 0.5 * D ** -0.5),
        'b_ada': _normal(ks[4], (L, 6 * D), 0.02),
        'norm1_g': 1.0 + _normal(ks[5], (L, D), 0.02),
        'w_in': _normal(ks[6], (L, D, IN_COLS), D ** -0.5),
        'q_a_norm_g': 1.0 + _normal(ks[7], (L, Q_LORA), 0.02),
        'w_uq': _normal(ks[8], (L, Q_LORA, H * QK_HEAD), Q_LORA ** -0.5),
        'kv_a_norm_g': 1.0 + _normal(ks[9], (L, KV_LORA), 0.02),
        'w_ukv': _normal(ks[10], (L, KV_LORA, H * (QK_NOPE + V_HEAD)), KV_LORA ** -0.5),
        'q_norm_g': 1.0 + _normal(ks[11], (L, QK_HEAD), 0.02),
        'k_norm_g': 1.0 + _normal(ks[12], (L, QK_HEAD), 0.02),
        'w_o_attn': _normal(ks[13], (L, H * V_HEAD, D), (H * V_HEAD) ** -0.5),
        'conv_w': _normal(ks[14], (L, CONV_WIDTH, LRU_WIDTH), CONV_WIDTH ** -0.5),
        'conv_b': _normal(ks[15], (L, LRU_WIDTH), 0.02),
        'w_rg': _normal(ks[16], (L, LRU_BLOCKS, LRU_BW, LRU_BW), LRU_BW ** -0.5),
        'b_rg': _normal(ks[17], (L, LRU_WIDTH), 0.02),
        'w_ig': _normal(ks[18], (L, LRU_BLOCKS, LRU_BW, LRU_BW), LRU_BW ** -0.5),
        'b_ig': _normal(ks[19], (L, LRU_WIDTH), 0.02),
        'lru_lambda': lru_lambda,
        'w_o_lru': _normal(ks[22], (L, LRU_WIDTH, D), LRU_WIDTH ** -0.5),
        'w_out': _normal(ks[23], (L, D, D), D ** -0.5),
        'norm2_g': 1.0 + _normal(ks[24], (L, D), 0.02),
        'w_query': _normal(ks[25], (L, D, PEER_HEADS * PEER_DKEY), D ** -0.5),
        'sub_keys': _normal(ks[26], (L, PEER_HEADS, 2, N_KEYS, PEER_HALF), PEER_HALF ** -0.5),
        'expert_u': _normal(ks[27], (L, N_EXPERTS, D), D ** -0.5),
        'expert_v': _normal(ks[28], (L, N_EXPERTS, D), PEER_HEADS ** -0.5),
    }

def first_block(x, c, positions, w_ada, b_ada, norm1_g, w_in, q_a_norm_g, w_uq, kv_a_norm_g,
              w_ukv, q_norm_g, k_norm_g, w_o_attn, conv_w, conv_b, w_rg, b_rg, w_ig, b_ig,
              lru_lambda, w_o_lru, w_out, norm2_g, w_query, sub_keys, expert_u, expert_v):
    cs = jax.nn.silu(c)
    for l in range(DEPTH):
        mod = cs @ w_ada[l] + b_ada[l]
        shift1, scale1, gate1, shift2, scale2, gate2 = [m[:, None, :] for m in jnp.split(mod, 6, axis=-1)]
        h = rms_norm(x, norm1_g[l]) * (1 + scale1) + shift1
        proj = h @ w_in[l]
        c_q, c_kv, k_rope, lru_x, lru_gate, merge_logits = jnp.split(proj, IN_SPLITS, axis=-1)
        attn = mla_attention(c_q, c_kv, k_rope, positions, q_a_norm_g[l], w_uq[l],
                             kv_a_norm_g[l], w_ukv[l], q_norm_g[l], k_norm_g[l])
        rec = rg_lru_branch(lru_x, lru_gate, conv_w[l], conv_b[l], w_rg[l], b_rg[l],
                            w_ig[l], b_ig[l], lru_lambda[l])
        g_attn, g_rec = jnp.split(jax.nn.sigmoid(merge_logits), 2, axis=-1)
        y = g_attn * (attn @ w_o_attn[l]) + g_rec * (rec @ w_o_lru[l])
        x = x + gate1 * (y @ w_out[l])
        h2 = rms_norm(x, norm2_g[l]) * (1 + scale2) + shift2
        x = x + gate2 * peer_ffn(h2, w_query[l], sub_keys[l], expert_u[l], expert_v[l])
    return x


N_HEADS_ATTN = 8
HEAD_DIM = 64
ATTN_WIDTH = N_HEADS_ATTN * HEAD_DIM
MOBA_BLOCK = 256
MOBA_TOPK = 3
Q_CHUNK = 32
ROPE_THETA_2 = 500000.0
ROT_DIM = HEAD_DIM // 4
CONV_WIDTH_2 = 512
CONV_K = 3
N_BRANCH = 2
IN_COLS_2 = 3 * ATTN_WIDTH + 3 * CONV_WIDTH_2 + N_BRANCH * D_MODEL
N_GROUPS = 4
EXPERTS_PER_GROUP = 8
N_EXPERTS_2 = N_GROUPS * EXPERTS_PER_GROUP
TOPK_IN_GROUP = 2
D_EXPERT = 512
MOE_BLOCK = 128
N_MOD = 6


def rms_norm_2(x, g):
    xf = x.astype(jnp.float32)
    y = xf * lax.rsqrt(jnp.mean(xf * xf, axis=-1, keepdims=True) + EPS)
    return (y * g.astype(jnp.float32)).astype(x.dtype)

def modulate(h, shift, scale):
    return h * (1 + scale[:, None, :]) + shift[:, None, :]

def rope_tables(seq_len, dtype):
    pos = jnp.arange(seq_len, dtype=jnp.float32)
    inv_freq = ROPE_THETA_2 ** (-jnp.arange(0, ROT_DIM, 2, dtype=jnp.float32) / ROT_DIM)
    ang = pos[:, None] * inv_freq[None, :]
    return jnp.cos(ang).astype(dtype), jnp.sin(ang).astype(dtype)

def partial_rope(x, cos, sin):
    half = ROT_DIM // 2
    x1, x2, xp = x[..., :half], x[..., half:ROT_DIM], x[..., ROT_DIM:]
    return jnp.concatenate([x1 * cos - x2 * sin, x2 * cos + x1 * sin, xp], axis=-1)

def moba_attention(q, k, v):
    B, H, S, dh = q.shape
    nb = -(-S // MOBA_BLOCK)
    pad = nb * MOBA_BLOCK - S
    kb = jnp.pad(k, ((0, 0), (0, 0), (0, pad), (0, 0))).reshape(B, H, nb, MOBA_BLOCK, dh)
    vb = jnp.pad(v, ((0, 0), (0, 0), (0, pad), (0, 0))).reshape(B, H, nb, MOBA_BLOCK, dh)
    kmean = jnp.mean(kb.astype(jnp.float32), axis=3)
    topk = min(MOBA_TOPK, nb)
    scale = HEAD_DIM ** -0.5
    b_ix = jnp.arange(B)[:, None, None, None]
    h_ix = jnp.arange(H)[None, :, None, None]
    blk_ids = jnp.arange(nb)
    t_in_blk = jnp.arange(MOBA_BLOCK)

    def chunk(ci):
        q0 = ci * Q_CHUNK
        qc = lax.dynamic_slice_in_dim(q, q0, Q_CHUNK, axis=2)
        qpos = q0 + jnp.arange(Q_CHUNK)
        cur = q0 // MOBA_BLOCK
        gate = jnp.einsum('bhqd,bhnd->bhqn', qc.astype(jnp.float32), kmean)
        gate = jnp.where(blk_ids < cur, gate, -jnp.inf)
        _, sel = lax.top_k(gate, topk)
        sel_valid = jnp.arange(topk) < cur
        k_sel = kb[b_ix, h_ix, sel]
        v_sel = vb[b_ix, h_ix, sel]
        s_sel = jnp.einsum('bhqd,bhqntd->bhqnt', qc, k_sel).astype(jnp.float32) * scale
        s_sel = jnp.where(sel_valid[:, None], s_sel, -jnp.inf)
        k_own = lax.dynamic_index_in_dim(kb, cur, axis=2, keepdims=False)
        v_own = lax.dynamic_index_in_dim(vb, cur, axis=2, keepdims=False)
        s_own = jnp.einsum('bhqd,bhtd->bhqt', qc, k_own).astype(jnp.float32) * scale
        kpos = cur * MOBA_BLOCK + t_in_blk
        s_own = jnp.where(kpos[None, :] <= qpos[:, None], s_own, -jnp.inf)
        logits = jnp.concatenate([s_sel.reshape(B, H, Q_CHUNK, topk * MOBA_BLOCK), s_own], axis=-1)
        p = jax.nn.softmax(logits, axis=-1).astype(v.dtype)
        p_sel = p[..., :topk * MOBA_BLOCK].reshape(B, H, Q_CHUNK, topk, MOBA_BLOCK)
        p_own = p[..., topk * MOBA_BLOCK:]
        return (jnp.einsum('bhqnt,bhqntd->bhqd', p_sel, v_sel)
                + jnp.einsum('bhqt,bhtd->bhqd', p_own, v_own))

    out = lax.map(chunk, jnp.arange(S // Q_CHUNK))
    return out.transpose(1, 2, 0, 3, 4).reshape(B, H, S, dh)

def short_gated_conv(xb, bg, cg, conv_w, conv_b):
    u = cg * xb
    y = lax.conv_general_dilated(u, conv_w[:, None, :], window_strides=(1,), padding=[(CONV_K - 1, 0)],
                                 dimension_numbers=('NWC', 'WIO', 'NWC'), feature_group_count=CONV_WIDTH_2)
    return bg * (y + conv_b)

def hierarchical_moe(h, w_rg, b_rg, w_re, b_re, w1, w3, w2):
    B, S, D = h.shape
    T = B * S
    xt = h.reshape(T, D)
    g_logits = (xt @ w_rg).astype(jnp.float32) + b_rg.astype(jnp.float32)
    g_prob = jax.nn.softmax(g_logits, axis=-1)
    g_idx = jnp.argmax(g_logits, axis=-1)
    g_w = jnp.take_along_axis(g_prob, g_idx[:, None], axis=-1)
    e_logits = ((xt @ w_re).astype(jnp.float32) + b_re.astype(jnp.float32)).reshape(T, N_GROUPS, EXPERTS_PER_GROUP)
    e_logits = jnp.take_along_axis(e_logits, g_idx[:, None, None], axis=1)[:, 0]
    e_val, e_loc = lax.top_k(e_logits, TOPK_IN_GROUP)
    e_w = jax.nn.softmax(e_val, axis=-1) * g_w
    e_id = g_idx[:, None].astype(jnp.int32) * EXPERTS_PER_GROUP + e_loc.astype(jnp.int32)

    n_assign = T * TOPK_IN_GROUP
    flat_e = e_id.reshape(-1)
    flat_w = e_w.reshape(-1)
    order = jnp.argsort(flat_e)
    sorted_e = flat_e[order]
    counts = jnp.bincount(flat_e, length=N_EXPERTS_2)
    padded = (counts + MOE_BLOCK - 1) // MOE_BLOCK * MOE_BLOCK
    start = jnp.cumsum(counts) - counts
    pad_end = jnp.cumsum(padded)
    pad_start = pad_end - padded
    dest = pad_start[sorted_e] + (jnp.arange(n_assign) - start[sorted_e])
    n_pad = (-(-n_assign // MOE_BLOCK) + N_EXPERTS_2) * MOE_BLOCK
    n_blocks = n_pad // MOE_BLOCK
    tok = jnp.full((n_pad,), T, jnp.int32).at[dest].set((order // TOPK_IN_GROUP).astype(jnp.int32))
    wpad = jnp.zeros((n_pad,), jnp.float32).at[dest].set(flat_w[order])
    blk_start = jnp.arange(n_blocks) * MOE_BLOCK
    blk_expert = jnp.minimum(jnp.sum(pad_end[None, :] <= blk_start[:, None], axis=-1), N_EXPERTS_2 - 1)
    x_ext = jnp.concatenate([xt, jnp.zeros((1, D), xt.dtype)], axis=0)
    xs = x_ext[tok].reshape(n_blocks, MOE_BLOCK, D)

    def expert_block(args):
        xb, e = args
        hid = jax.nn.silu(xb @ w1[e]) * (xb @ w3[e])
        return hid @ w2[e]

    ys = lax.map(expert_block, (xs, blk_expert)).reshape(n_pad, D)
    ys = ys * wpad[:, None].astype(ys.dtype)
    out = jnp.zeros((T + 1, D), ys.dtype).at[tok].add(ys)[:T]
    return out.reshape(B, S, D)

def second_inputs(seed: int = 0) -> dict:
    key = jax.random.key(seed)
    ks = jax.random.split(key, 24)
    L, D = DEPTH, D_MODEL
    f32 = jnp.float32
    nrm = lambda k, shape, s: jax.random.normal(k, shape, f32) * s
    return {
        "x": nrm(ks[0], (BATCH, SEQ, D), 1.0),
        "c": nrm(ks[1], (BATCH, D), 1.0),
        "w_ada": nrm(ks[2], (L, D, N_MOD * D), 0.5 * D ** -0.5),
        "b_ada": nrm(ks[3], (L, N_MOD * D), 0.02),
        "g_norm1": 1.0 + nrm(ks[4], (L, D), 0.02),
        "g_norm2": 1.0 + nrm(ks[5], (L, D), 0.02),
        "w_in": nrm(ks[6], (L, D, IN_COLS_2), D ** -0.5),
        "g_q": 1.0 + nrm(ks[7], (L, HEAD_DIM), 0.02),
        "g_k": 1.0 + nrm(ks[8], (L, HEAD_DIM), 0.02),
        "conv_w": nrm(ks[9], (L, CONV_K, CONV_WIDTH_2), CONV_K ** -0.5),
        "conv_b": nrm(ks[10], (L, CONV_WIDTH_2), 0.02),
        "w_pa": nrm(ks[11], (L, ATTN_WIDTH, D), ATTN_WIDTH ** -0.5),
        "w_pb": nrm(ks[12], (L, CONV_WIDTH_2, D), CONV_WIDTH_2 ** -0.5),
        "w_o": nrm(ks[13], (L, D, D), D ** -0.5),
        "w_rg": nrm(ks[14], (L, D, N_GROUPS), D ** -0.5),
        "b_rg": nrm(ks[15], (L, N_GROUPS), 0.01),
        "w_re": nrm(ks[16], (L, D, N_EXPERTS_2), D ** -0.5),
        "b_re": nrm(ks[17], (L, N_EXPERTS_2), 0.01),
        "w1": nrm(ks[18], (L, N_EXPERTS_2, D, D_EXPERT), D ** -0.5),
        "w3": nrm(ks[19], (L, N_EXPERTS_2, D, D_EXPERT), D ** -0.5),
        "w2": nrm(ks[20], (L, N_EXPERTS_2, D_EXPERT, D), D_EXPERT ** -0.5),
    }

def second_block(x, c, w_ada, b_ada, g_norm1, g_norm2, w_in, g_q, g_k, conv_w, conv_b,
              w_pa, w_pb, w_o, w_rg, b_rg, w_re, b_re, w1, w3, w2):
    B, S, D = x.shape
    cos, sin = rope_tables(S, x.dtype)
    splits = [ATTN_WIDTH, 2 * ATTN_WIDTH, 3 * ATTN_WIDTH,
              3 * ATTN_WIDTH + CONV_WIDTH_2, 3 * ATTN_WIDTH + 2 * CONV_WIDTH_2, 3 * ATTN_WIDTH + 3 * CONV_WIDTH_2]
    for l in range(DEPTH):
        mod = jax.nn.silu(c) @ w_ada[l] + b_ada[l]
        sh1, sc1, ga1, sh2, sc2, ga2 = jnp.split(mod, N_MOD, axis=-1)

        h = modulate(rms_norm_2(x, g_norm1[l]), sh1, sc1)
        z = h @ w_in[l]
        q, k, v, xb, bg, cg, gates = jnp.split(z, splits, axis=-1)
        to_heads = lambda t: t.reshape(B, S, N_HEADS_ATTN, HEAD_DIM).transpose(0, 2, 1, 3)
        q = partial_rope(rms_norm_2(to_heads(q), g_q[l]), cos, sin)
        k = partial_rope(rms_norm_2(to_heads(k), g_k[l]), cos, sin)
        v = to_heads(v)
        y_a = moba_attention(q, k, v).transpose(0, 2, 1, 3).reshape(B, S, ATTN_WIDTH)
        y_b = short_gated_conv(xb, bg, cg, conv_w[l], conv_b[l])
        gate_a, gate_b = jnp.split(jax.nn.sigmoid(gates), N_BRANCH, axis=-1)
        merged = gate_a * (y_a @ w_pa[l]) + gate_b * (y_b @ w_pb[l])
        x = x + ga1[:, None, :] * (merged @ w_o[l])

        h2 = modulate(rms_norm_2(x, g_norm2[l]), sh2, sc2)
        x = x + ga2[:, None, :] * hierarchical_moe(h2, w_rg[l], b_rg[l], w_re[l], b_re[l], w1[l], w3[l], w2[l])
    return x


def setup_inputs(seed=0):
    out = dict(first_inputs(seed))
    for name, value in second_inputs(seed + 1).items():
        if name != "x":
            out[name + "_2"] = value
    return out


def reference(
    x, c, positions, w_ada, b_ada, norm1_g, w_in, q_a_norm_g, w_uq, kv_a_norm_g, w_ukv,
    q_norm_g, k_norm_g, w_o_attn, conv_w, conv_b, w_rg, b_rg, w_ig, b_ig, lru_lambda, w_o_lru,
    w_out, norm2_g, w_query, sub_keys, expert_u, expert_v, c_2, w_ada_2, b_ada_2, g_norm1_2,
    g_norm2_2, w_in_2, g_q_2, g_k_2, conv_w_2, conv_b_2, w_pa_2, w_pb_2, w_o_2, w_rg_2, b_rg_2,
    w_re_2, b_re_2, w1_2, w3_2, w2_2,
):
    x = first_block(
        x, c, positions, w_ada, b_ada, norm1_g, w_in, q_a_norm_g, w_uq, kv_a_norm_g, w_ukv,
        q_norm_g, k_norm_g, w_o_attn, conv_w, conv_b, w_rg, b_rg, w_ig, b_ig, lru_lambda,
        w_o_lru, w_out, norm2_g, w_query, sub_keys, expert_u, expert_v,
    )
    return second_block(
        x, c_2, w_ada_2, b_ada_2, g_norm1_2, g_norm2_2, w_in_2, g_q_2, g_k_2, conv_w_2,
        conv_b_2, w_pa_2, w_pb_2, w_o_2, w_rg_2, b_rg_2, w_re_2, b_re_2, w1_2, w3_2, w2_2,
    )


_drawn_inputs = setup_inputs


def setup_inputs(seed=0):
    import zlib

    import numpy as np

    out = dict(_drawn_inputs(seed))
    spreads = {}
    factors = {'norm1_g': 6.223,
     'q_a_norm_g': 8.0,
     'kv_a_norm_g': 8.0,
     'q_norm_g': 8.0,
     'k_norm_g': 8.0,
     'conv_b': 4.096,
     'b_rg': 8.0,
     'b_ig': 7.972,
     'norm2_g': 15.865,
     'g_norm1_2': 5.715,
     'g_norm2_2': 28.944,
     'g_q_2': 64.0,
     'g_k_2': 64.0,
     'conv_b_2': 64.0,
     'b_rg_2': 64.0,
     'b_re_2': 64.0}
    for name, (base, spread) in spreads.items():
        noise = np.random.default_rng([zlib.crc32(name.encode()), seed]).standard_normal(out[name].shape)
        drawn = base * np.exp(spread * noise) if base else spread * noise
        out[name] = __import__('jax').numpy.asarray(drawn.astype(out[name].dtype))
    for name, factor in factors.items():
        out[name] = (out[name] * factor).astype(out[name].dtype)
    return out
```

```python
import math
from contextlib import ExitStack

import numpy as np
import concourse.bass as bass
from concourse import mybir
from concourse.alu_op_type import AluOpType as ALU

F32 = mybir.dt.float32
I32 = mybir.dt.int32
U32 = mybir.dt.uint32
ACT = mybir.ActivationFunctionType
AX = mybir.AxisListType

P = 128
T = 256
TT = T // P
D = 1024
DC = D // P
EPS = 1e-6
BIG = 3.4028234663852886e38
HEADS = 8
HV = 64
HD1, ROT1 = 96, 32
HD2, ROT2 = 64, 16
QC, KVC, KRC = 256, 128, 32
PH = 8
NKEY = 128
TOPK = 16
NEXP = 32
DE = 512
SLOTS = 32
OVER = 16
NSLOT = 6
SLAB = 4096
NROW = 8
KEY_OUT = -1.0e6


def columns_layout():
    sizes = [("c", 8), ("b_ada", 48), ("norm1_g", 8), ("norm2_g", 8), ("q_a_norm_g", 2), ("kv_a_norm_g", 1),
             ("conv_w", 32), ("conv_b", 8), ("b_rg", 8), ("b_ig", 8), ("lru_lambda", 8),
             ("c_2", 8), ("b_ada_2", 48), ("g_norm1_2", 8), ("g_norm2_2", 8), ("conv_w_2", 12), ("conv_b_2", 4)]
    at, out = 0, {}
    for name, n in sizes:
        out[name] = (at, at + n)
        at += n
    return out, at


def rows_layout():
    sizes = [("q_norm_g", 96), ("k_norm_g", 96), ("g_q_2", 64), ("g_k_2", 64), ("b_rg_2", 4), ("b_re_2", 32)]
    at, out = 0, {}
    for name, n in sizes:
        out[name] = (at, at + n)
        at += n
    return out, at


def constants():
    p = np.arange(P)[:, None].astype(np.float64)
    j = np.arange(P)[None, :].astype(np.float64)
    parts = []
    parts.append(("ident", (p == j)))
    parts.append(("ones", np.ones((P, P))))
    parts.append(("before", (p < j)))
    full = np.full((P, P), BIG)
    chunked = np.where(np.floor(j / 64) <= np.floor(p / 64), BIG, -BIG)
    causal = np.where(j <= p, BIG, -BIG)
    parts.append(("bound1", np.concatenate([chunked, full, chunked], 1)))
    parts.append(("bound2", np.concatenate([causal, full, causal], 1)))
    parts.append(("slot4", np.broadcast_to(np.arange(P) % SLOTS, (P, P))))
    fold = np.zeros((P, 2 * SLOTS))
    for q in range(P):
        fold[q, (q // 64) * SLOTS + q % SLOTS] = 1
    parts.append(("fold", fold))
    parts.append(("iota32", np.broadcast_to(np.arange(32), (P, 32))))
    freq1 = (1.0 / (np.float32(10000.0) ** (np.arange(0, ROT1, 2, dtype=np.float32) / np.float32(ROT1)))).astype(np.float32)
    parts.append(("freq", np.broadcast_to(freq1, (P, 16))))
    freq2 = (np.float32(500000.0) ** (-np.arange(0, ROT2, 2, dtype=np.float32) / np.float32(ROT2))).astype(np.float32)
    ang = (np.arange(T, dtype=np.float32)[:, None] * freq2[None, :]).astype(np.float32).reshape(TT, P, 8).transpose(1, 0, 2)
    parts.append(("cos2", np.cos(ang.astype(np.float64)).reshape(P, 16)))
    parts.append(("sin2", np.sin(ang.astype(np.float64)).reshape(P, 16)))
    at, where = 0, {}
    for name, a in parts:
        where[name] = (at, at + a.shape[1])
        at += a.shape[1]
    return where, np.ascontiguousarray(np.concatenate([np.asarray(a, np.float32) for _, a in parts], 1))


def attention_plan(tag):
    out = [(f"{tag}qT{i}", "A" if i % 2 else "D", []) for i in range(8)]
    out.append((f"{tag}S0", "D", []))
    for h in range(HEADS):
        if h + 1 < HEADS:
            out.append((f"{tag}S{h + 1}", "D", []))
        out.append((f"{tag}PT{h}", "A", []))
        if h % 4 == 3:
            out.append((f"{tag}O{h // 4}", "D", []))
    out += [(f"{tag}AT{t}", "A", []) for t in range(TT)]
    return out


def make_plan():
    pl = [("ss1", "D", []), ("ada0", "A", [f"ada{i}" for i in range(4)]), ("adaT0", "D", [])]
    pl += [("cq", "D", []), ("ckr", "D", ["in_small"])]
    pl += [(f"lx{i}", "D", [f"in_lx{i // 2}"] if i % 2 else []) for i in range(4)]
    pl += [("sscq", "D", [])]
    pl += [(f"qp{t}{i}", "A", []) for t in range(2) for i in range(2)]
    pl += [(f"kv{t}{i}", "D", ["qkv"] if (t, i) == (1, 1) else []) for t in range(2) for i in range(2)]
    pl += [(f"lg{i}", "A", [f"in_lg{i // 2}"] if i % 2 else []) for i in range(4)]
    for r in (1, 2):
        pl += [(f"ada{r}", "A", [f"ada{i}" for i in range(4 * r, 4 * r + 4)]), (f"adaT{r}", "D", [])]
    pl += [(f"lr{i}", "A", ["gates"] if i == 7 else []) for i in range(8)]
    turn = lambda r: [(f"bda{r}", "A", [f"bda{i}" for i in range(4 * r, 4 * r + 4)]), (f"bdaT{r}", "A", [])]
    pl += [(f"mg{i}", "A", [f"in_mg{i // 2}"] if i % 2 else []) for i in range(4)] + turn(0)
    pl += [(f"mg{i}", "A", [f"in_mg{i // 2}"] if i % 2 else []) for i in range(4, 8)] + turn(1)
    pl += attention_plan("a")
    pl += turn(2)
    pl += [(f"ya{i}", "D", ["o_attn"] if i == 3 else []) for i in range(4)]
    pl += [(f"yl{i}", "D", [f"o_lru{i // 2}"] if i % 2 else []) for i in range(4)]
    pl += [(f"xo{i}", "D", [f"w_out{i // 2}"] if i % 2 else []) for i in range(4)]
    pl += [("ss2", "D", [])]
    pl += [(f"pq{i}", "A", [f"w_query{i // 2}"] if i % 2 else []) for i in range(8)]
    pl += [(f"sc{t}{i}", "D" if i % 2 else "A", ["keys"] if (t, i) == (1, 3) else []) for t in range(2) for i in range(4)]
    pl += [(f"ht{i}", "A", []) for i in range(4)]
    pl += [(f"po{t}{i}", "D", []) for t in range(2) for i in range(2)]
    pl += [("ss3", "D", [])]
    pl += [(f"zq{t}", "A", []) for t in range(2)] 
    pl[-1] = (pl[-1][0], "A", ["in2_0"])
    pl += [("zk0", "D", []), ("zk1", "D", ["in2_1"]), ("zv0", "A", []), ("zv1", "A", ["in2_2"])]
    pl += [(f"zx{i}", "A", ["in2_3"] if i else []) for i in range(2)]
    pl += [(f"zb{i}", "A", ["in2_4"] if i else []) for i in range(2)]
    pl += [(f"zc{i}", "D", ["in2_5"] if i else []) for i in range(2)]
    pl += [(f"zg{i}", "A", [f"in2_{6 + i // 2}"] if i % 2 else []) for i in range(8)]
    pl += attention_plan("b")
    pl += [(f"wa{i}", "D", ["w_pa"] if i == 3 else []) for i in range(4)]
    pl += [(f"wb{i}", "D", ["w_pb"] if i == 3 else []) for i in range(4)]
    pl += [(f"xp{i}", "D", [f"w_o_2{i // 2}"] if i % 2 else []) for i in range(4)]
    pl += [("ss4", "D", [])]
    pl += [("rt0", "D", []), ("rt1", "D", []), ("cnt", "D", []), ("pos", "D", [])]
    pl += [(f"hu{i}", "A", []) for i in range(4)]
    return pl


def build(nc, g, out):
    ctx = ExitStack()
    with ctx:
        program(nc, g, out, ctx)


def program(nc, g, out, ctx):
    COL, NCOL = columns_layout()
    ROW, NROWV = rows_layout()
    CST = constants()[0]
    NCST = max(b for _, b in CST.values())

    def sb(name, shape, dt=F32):
        return ctx.enter_context(nc.sbuf_tensor(name, shape, dt))

    def sem(name):
        return ctx.enter_context(nc.semaphore(name))

    slabs = sb("weight_slabs", [P, NSLOT, SLAB])
    rows = sb("gathered_rows", [P, NROW, D])
    xT = sb("xT", [P, DC, T])
    hT = sb("hT", [P, DC, T])
    cols = sb("columns", [P, NCOL])
    rowv = sb("row_vectors", [P, NROWV])
    cst = sb("constants_sb", [P, NCST])
    mod = sb("modulation", [P, 2, 48])
    amul = sb("amul", [P, 4, DC])
    csb = sb("silu_c", [P, 2, DC, 32])
    ada_sb = sb("ada_sb", [P, 512])
    var = sb("var", [P, 512])
    std = sb("std", [P, 512])
    rst = sb("rstd", [P, 512])
    newt = sb("newton", [P, 512])
    posn = sb("positions_sb", [P, TT], I32)
    trig = sb("trig", [P, 6, 32])
    wroute = sb("w_route", [P, DC, 36])
    small = sb("small", [P, 16, 8])
    zero = sb("zero", [P, P])[:, :]
    posf = sb("positions_f32", [P, TT])
    tick0, tick = sb("tick_zero", [P, 1], I32), sb("tick", [P, 1], I32)
    idx_stage = sb("index_stage", [P, 2, TOPK], I32)
    work = sb("work", [P, 10324])

    def view(at, n, pat=None, **kw):
        a = work[:, at:at + n]
        return a.rearrange(pat, **kw) if pat else a

    rows_flat = rows[:, :, :].rearrange("p a b -> p (a b)")

    def C(name, n=None):
        a, b = COL[name]
        return cols[:, a:b] if n is None else cols[:, a + n:a + n + 1]

    def K(name):
        a, b = CST[name]
        return cst[:, a:b]

    def R(name):
        a, b = ROW[name]
        return rowv[:, a:b]

    ident, ones = K("ident"), K("ones")

    ps = [ctx.enter_context(nc.psum_tensor(f"bank{i}", [P, 512], F32)) for i in range(8)]

    PLAN = make_plan()
    INDEX = {name: n for n, (name, _, _) in enumerate(PLAN)}

    def evacs(engine, last_index):
        return sum(1 for _, e, _ in PLAN[:last_index + 1] if e == engine)

    chunk_ready = sem("chunk_ready")
    emptied = {"A": sem("chunk_emptied_by_scalar"), "D": sem("chunk_emptied_by_vector")}

    def bank(name):
        return ps[INDEX[name] % 8]

    def wait_emptied(eng, name):
        n = INDEX[name]
        e = PLAN[n][1]
        eng.wait_ge(emptied[e], evacs(e, n))

    NORMS = {n: i + 1 for i, n in enumerate(("n1", "lora", "aqk0", "aqk1", "n2", "n3", "bqk0", "bqk1", "n4"))}

    def cols_of(w, a, b):
        return w[:, a:b].rearrange("(c p) n -> p c n", p=P)

    def slab3(c, n):
        return lambda s: s[:, 0:c * n].rearrange("p (c n) -> p c n", n=n)

    A0 = QC + KVC + KRC
    LXC = A0 + D
    MGC = A0 + 2 * D
    SL = []
    SL += [(f"ada{i}", [(slab3(8, 512), cols_of(g["w_ada"], 512 * i, 512 * i + 512))]) for i in range(4)]
    SL += [("in_small", [(slab3(8, A0), cols_of(g["w_in"], 0, A0))])]
    SL += [(f"in_lx{i}", [(slab3(8, 512), cols_of(g["w_in"], A0 + 512 * i, A0 + 512 * i + 512))]) for i in range(2)]
    SL += [("qkv", [(slab3(2, 768), cols_of(g["w_uq"], 0, 768)),
                    (lambda s: s[:, 1536:2560].rearrange("p (c n) -> p c n", c=1), cols_of(g["w_ukv"], 0, 1024))])]
    SL += [(f"in_lg{i}", [(slab3(8, 512), cols_of(g["w_in"], LXC + 512 * i, LXC + 512 * i + 512))]) for i in range(2)]
    SL += [(f"ada{i}", [(slab3(8, 512), cols_of(g["w_ada"], 512 * i, 512 * i + 512))]) for i in range(4, 12)]
    SL += [("gates", [(slab3(8, 128), g["w_rg"].rearrange("n i o -> i n o")),
                      (lambda s: s[:, 1024:2048].rearrange("p (c n) -> p c n", c=8), g["w_ig"].rearrange("n i o -> i n o"))])]
    mg = [(f"in_mg{i}", [(slab3(8, 512), cols_of(g["w_in"], MGC + 512 * i, MGC + 512 * i + 512))]) for i in range(4)]
    bda = [(f"bda{i}", [(slab3(8, 512), cols_of(g["w_ada_2"], 512 * i, 512 * i + 512))]) for i in range(12)]
    SL += mg[0:2] + bda[0:4] + mg[2:4] + bda[4:12]
    SL += [("o_attn", [(slab3(4, 1024), cols_of(g["w_o_attn"], 0, 1024))])]
    SL += [(f"o_lru{i}", [(slab3(8, 512), cols_of(g["w_o_lru"], 512 * i, 512 * i + 512))]) for i in range(2)]
    SL += [(f"w_out{i}", [(slab3(8, 512), cols_of(g["w_out"], 512 * i, 512 * i + 512))]) for i in range(2)]
    SL += [(f"w_query{i}", [(slab3(8, 512), cols_of(g["w_query"], 512 * i, 512 * i + 512))]) for i in range(4)]
    SL += [("keys", [(slab3(16, 128), g["keysT"])])]
    SL += [(f"in2_{i}", [(slab3(8, 512), cols_of(g["w_in_2"], 512 * i, 512 * i + 512))]) for i in range(10)]
    SL += [("w_pa", [(slab3(4, 1024), cols_of(g["w_pa_2"], 0, 1024))]), ("w_pb", [(slab3(4, 1024), cols_of(g["w_pb_2"], 0, 1024))])]
    SL += [(f"w_o_2{i}", [(slab3(8, 512), cols_of(g["w_o_2"], 512 * i, 512 * i + 512))]) for i in range(2)]
    MOE0 = len(SL) % NSLOT
    for e in range(2):
        SL += [(f"moe{e}_w1", [(slab3(8, 512), cols_of(g["w1_2"][e], 0, DE))]), (f"moe{e}_w3", [(slab3(8, 512), cols_of(g["w3_2"][e], 0, DE))]),
               (f"moe{e}_w2", [(slab3(4, 1024), cols_of(g["w2_2"][e], 0, D))])]
    SLAB_AT = {name: n for n, (name, _) in enumerate(SL)}
    slab_done = {s: n for n, (_, _, done) in enumerate(PLAN) for s in done}
    loads_of_slot, slab_value = [0] * NSLOT, []
    for n, (_, dmas) in enumerate(SL):
        loads_of_slot[n % NSLOT] += 16 * len(dmas)
        slab_value.append(loads_of_slot[n % NSLOT])
    slab_loaded = [sem(f"slab{i}_loaded") for i in range(NSLOT)]

    inputs_in, consts_in = sem("inputs_in"), sem("consts_in")
    dve_step = sem("dve_step")
    act_step = sem("act_step")
    zero_ready = sem("zero_ready")
    silu_ready, square_ready = sem("silu_ready"), sem("square_ready")
    var_ready, std_ready = sem("var_ready"), sem("std_ready")
    scaled_ready, h_ready = sem("scaled_ready"), sem("h_ready")
    trig_arg, trig_done = sem("trig_arg"), sem("trig_done")
    lora_sq, lora_ready = sem("lora_squares"), sem("lora_ready")
    lam_exp = sem("lambda_exp")
    lru_const = sem("lru_constants")
    conv_ready = sem("conv_ready")
    gate_val = sem("gate_value")
    decay_ready, decay_sq = sem("decay_ready"), sem("one_minus_a2")
    input_scale = sem("input_scale")
    lru_root = sem("lru_root")
    rec_ready = sem("rec_ready")
    qk_in, qk_square, qk_ready = sem("qk_in"), sem("qk_square"), sem("qk_ready")
    bias_ready, exp_ready = sem("max_ready"), sem("exp_ready")
    y_ready, x_ready = sem("y_ready"), sem("x_ready")
    stored = sem("stored")
    best_ready, best_exp = sem("best_ready"), sem("best_exp")
    index_ready = sem("expert_index_ready")
    row_in = [sem(f"row{k}_gathered") for k in range(NROW)]
    row_free = [sem(f"row{k}_free") for k in range(NROW)]
    pool_tick, index_staged = sem("pool_tick"), sem("index_staged")
    sum_inverse, route_step = sem("sum_inverse"), sem("route_step")
    gelu_ready, weight_ready = sem("gelu_ready"), sem("expert_weight_ready")
    diag_ready = sem("diag_ready")
    acc_step, sum_ready = sem("vector_sum_step"), sem("tensor_sum_ready")
    peer_out = sem("peer_rows_ready")
    routed_ready, route_exp = sem("routed_ready"), sem("route_exp")
    assign_ready, table_ready = sem("assignment_ready"), sem("block_table_ready")
    m_w13, m_x4, m_fold, m_xt = sem("moe_w13_done"), sem("moe_picked"), sem("moe_hidden_folded"), sem("moe_x_folded")
    m_pwt, m_w2, m_comb = sem("moe_place_turned"), sem("moe_w2_done"), sem("moe_combined")
    pick_ready, x4_out, xt_out = sem("moe_pick_ready"), sem("moe_x4_out"), sem("moe_xt_out")
    hp_out, silu_out, hid_ready = sem("moe_hp_out"), sem("moe_silu_out"), sem("moe_hidden_ready")
    place_ready, placeT_out = sem("moe_place_ready"), sem("moe_placeT_out")
    y0_out, y1_out = sem("moe_y0_out"), sem("moe_y1_out")

    lx = view(0, DC * (T + 3), "p (c t) -> p c t", c=DC)
    lxm = view(0, 2048, "p (c t) -> p c t", c=DC)
    xc = view(2072, 2048, "p (c t) -> p c t", c=DC)
    dec = rows_flat[:, 4096:6144].rearrange("p (c t) -> p c t", c=DC)
    gate = view(4120, 2048, "p (c t) -> p c t", c=DC)
    merge = view(6168, 4096, "p (c t) -> p c t", c=2 * DC)
    cq = rows_flat[:, 6400:6912].rearrange("p (c t) -> p c t", c=2)
    ckv = rows_flat[:, 6912:7168]
    krope = view(6936, 64, "p (t r) -> p t r", t=TT)
    gexp = rows_flat[:, 7168:8192].rearrange("p (b n) -> p b n", b=2)
    gth = rows_flat[:, 6400:6912].rearrange("p (b n) -> p b n", b=2)
    ga2 = rows_flat[:, 6912:7168]
    lsq = view(6168, 768, "p (c t) -> p c t", c=3)
    qk1 = rows_flat[:, 0:3072].rearrange("p (t h d) -> p t h d", t=TT, h=16)
    qk2 = rows_flat[:, 0:2048].rearrange("p (t h d) -> p t h d", t=TT, h=16)
    vv = rows_flat[:, 3072:4096].rearrange("p (t n) -> p t n", t=TT)
    qkT = rows_flat[:, 4096:8192].rearrange("p (h t) -> p h t", h=16)
    sq1 = rows_flat[:, 4096:5632].rearrange("p (h d) -> p h d", h=16)
    sq2 = rows_flat[:, 4096:5120].rearrange("p (h d) -> p h d", h=16)
    rot = [newt[:, 256:512]] + [rows_flat[:, 5632 + 256 * i:5888 + 256 * i] for i in range(3)]
    sm = view(2072, 768, "p (b n) -> p b n", b=2)
    pb = view(2840, 768, "p (b n) -> p b n", b=2)
    ptb = view(0, 1536, "p (b n) -> p b n", b=4)
    nmax = view(10264, 16, "p (h t) -> p h t", h=HEADS)
    rsum = view(10280, 16, "p (t h) -> p t h", t=TT)
    rinv = view(10296, 16, "p (t h) -> p t h", t=TT)
    att = rows_flat[:, 0:1024].rearrange("p (t n) -> p t n", t=TT)
    attT = rows_flat[:, 1024:2048].rearrange("p (c t) -> p c t", c=4)
    yT = lxm
    ytmp = view(2072, 1024, "p (b n) -> p b n", b=2)
    sqx = view(2072, 2048, "p (c t) -> p c t", c=DC)
    cx = view(0, 4 * (T + 2), "p (c t) -> p c t", c=4)
    zb = view(4120, 1024, "p (c t) -> p c t", c=4)
    zx = view(2072, 1024, "p (c t) -> p c t", c=4)
    cv = view(3096, 1024, "p (c t) -> p c t", c=4)
    qT = rows_flat[:, 0:4096].rearrange("p (c t) -> p c t", c=16)
    sc = view(0, 4096, "p (t n) -> p t n", t=TT)
    htok = view(4096, 2048, "p (t n) -> p t n", t=TT)
    sc_flat = view(0, 4096)
    cand = view(6144, 256)
    hot = view(6400, 512, "p (s k j) -> p s k j", s=2, k=TOPK)
    carrier = view(9188, 1)
    stage = view(6912, 256)
    accv = view(7168, 1024)
    diag = view(8192, 640, "p (k n) -> p k n", k=5)
    peer = view(0, 2048, "p (t n) -> p t n", t=TT)
    stop_ = view(8832, 32, "p (g k) -> p g k", g=2)
    itop = view(8864, 32, "p (g k) -> p g k", g=2).bitcast(U32)
    itopf = view(8896, 32, "p (g k) -> p g k", g=2)
    best = view(8928, 16)
    bpos = view(8944, 16).bitcast(U32)
    bhalf = view(8960, 32, "p (s n) -> p s n", s=2).bitcast(U32)
    bhalff = view(8992, 32, "p (s n) -> p s n", s=2)
    ihalf = view(9024, 32, "p (s n) -> p s n", s=2)
    eidx = view(9056, 32, "p (b n) -> p b n", b=2).bitcast(I32)
    gsoft = view(9088, 32, "p (b n) -> p b n", b=2)
    gsum = view(9120, 4, "p (b n) -> p b n", b=2)
    dots = view(9124, 32, "p (b n) -> p b n", b=2)
    wexp = view(9156, 32, "p (b n) -> p b n", b=2)
    logit = view(6144, 72, "p (t n) -> p t n", t=TT)
    gpad = view(6216, 16, "p (t n) -> p t n", t=TT)
    top8 = view(6232, 32, "p (a t n) -> p a t n", a=2, t=TT)
    idx8 = view(6264, 32, "p (a t n) -> p a t n", a=2, t=TT).bitcast(U32)
    idxf = view(6296, 32, "p (a t n) -> p a t n", a=2, t=TT)
    gmask = view(6328, 8, "p (t n) -> p t n", t=TT)
    emask = view(6336, 64, "p (t n) -> p t n", t=TT)
    gate2v = view(6400, 16, "p (t n) -> p t n", t=TT)
    assign = view(6416, 64, "p (t n) -> p t n", t=TT)
    awt = view(6480, 64, "p (t n) -> p t n", t=TT)
    hot1 = view(6544, 32)
    extra = view(6576, 32)
    cum = view(6608, 32)
    start = view(6640, 32)
    kplus = view(6672, 64, "p (t n) -> p t n", t=TT)
    oh = view(6736, 512, "p (o e) -> p o e", o=OVER)
    oh2 = view(7248, 512, "p (o e) -> p o e", o=OVER)
    oact = view(7760, 16)
    keyb = view(7776, 100, "p (t n) -> p t n", t=TT)
    wb = view(7876, 100, "p (t n) -> p t n", t=TT)
    etabf = view(7976, 52)
    etab = view(8028, 52).bitcast(I32)
    npair_sb = etab[:, 50:51]
    oshift = view(8080, 16)
    gexp4 = view(8096, 8, "p (t n) -> p t n", t=TT)
    cntv = view(8104, 32)
    pick = view(8192, 128, "p (b t s) -> p b t s", b=2, t=TT)
    x4s = view(2816, 512)
    xts = view(3328, 512, "p (b c a s) -> p b c a s", b=2, c=4, a=2)
    hps = view(8320, 512)
    sil = view(8832, 128, "p (c s) -> p c s", c=4)
    hts = view(8960, 128, "p (c s) -> p c s", c=4)
    place = view(2560, 256, "p (t n) -> p t n", t=TT)
    placeT = view(2048, 512, "p (b n) -> p b n", b=2)
    y4s = view(0, 2048, "p (b n) -> p b n", b=2)
    outT = hT[:, :, :]

    V_TENSOR = [0, 1, 3, 4, 6]
    V_VECTOR = [2, 5, 7]
    ROUTE = 18

    block = ctx.enter_context(nc.Block())

    @block.sync
    def _(sp):
        sp.dma_start(xT[:, :, :], g["xT"]).then_inc(inputs_in, 16)
        sp.dma_start(cols[:, :], g["columns"]).then_inc(inputs_in, 16)
        sp.dma_start(posn[:, :], g["pos"]).then_inc(inputs_in, 16)
        sp.dma_start(cst[:, :], g["constants"]).then_inc(consts_in, 16)
        sp.dma_start(rowv[:, :], g["rows"].partition_broadcast(P)).then_inc(consts_in, 16)
        sp.dma_start(wroute[:, :, :], cols_of(g["w_route"], 0, 36)).then_inc(consts_in, 16)
        for n, (name, dmas) in enumerate(SL):
            if n >= NSLOT and SL[n - NSLOT][0] in slab_done:
                sp.wait_ge(chunk_ready, slab_done[SL[n - NSLOT][0]] + 1)
            for dst, src in dmas:
                sp.dma_start(dst(slabs[:, n % NSLOT, :]), src).then_inc(slab_loaded[n % NSLOT], 16)
        sp.wait_ge(table_ready, 1)
        npair = sp.value_load(npair_sb[0:1, :], min_val=NEXP // 2, max_val=(NEXP + OVER) // 2)
        with sp.Fori(1, npair) as i:
            for par in range(2):
                e = sp.value_load(etab[0:1, bass.ds(i * 2 + par, 1)], min_val=0, max_val=NEXP - 1)
                base = MOE0 + 3 * par
                for w in range(3):
                    slot = (base + w) % NSLOT
                    sp.wait_ge(m_w2 if w == 2 else m_w13, (i * 2 + par - 1) * (2 if w == 2 else 1))
                    name = ("w1_2", "w3_2", "w2_2")[w]
                    src = g[name][bass.ds(e, 1)].rearrange("o (c p) n -> p (o c) n", p=P)
                    sp.dma_start(slab3(8, 512)(slabs[:, slot, :]) if w < 2 else slab3(4, 1024)(slabs[:, slot, :]),
                                 src).then_inc(slab_loaded[slot], 16)
        sp.wait_ge(x_ready, 4)
        sp.dma_start(out, outT[:, :, :]).then_inc(stored, 16)
        sp.wait_ge(stored, 16)

    @block.tensor
    def _(pe):
        def begin(name):
            n = INDEX[name]
            if n >= 8:
                e = PLAN[n - 8][1]
                pe.wait_ge(emptied[e], evacs(e, n - 8))
            return ps[n % 8]

        def slab(name):
            n = SLAB_AT[name]
            pe.wait_ge(slab_loaded[n % NSLOT], slab_value[n])
            return slabs[:, n % NSLOT, :]

        def done(ins):
            ins.then_inc(chunk_ready, 1)

        def feature_pair(name, w, f0, rhs, nk, finish=True):
            b = begin(name)
            for t in range(2):
                for k in range(nk):
                    last = nc.tensor.matmul(b[:, t * T:(t + 1) * T], w[:, k, f0 + t * P:f0 + (t + 1) * P], rhs[:, k, :],
                                            start=(k == 0), stop=(k == nk - 1))
            done(last)

        def ada(name, prefix, r, which):
            ws = [slab3(8, 512)(slab(f"{prefix}{4 * r + j}")) for j in range(4)]
            b = begin(name)
            for k in range(DC):
                for j in range(4):
                    last = nc.tensor.matmul(b[32 * j:32 * j + 32, :], csb[:, which, k, :], ws[j][:, k, :],
                                            start=(k == 0), stop=(k == DC - 1), tile_position=(0, 32 * j))
            done(last)

        def turn4(name, src, ready=None):
            b = begin(name)
            if ready:
                pe.wait_ge(*ready)
            for q in range(4):
                last = nc.tensor.transpose(b[:, q * P:(q + 1) * P], src(q), ident)
            done(last)

        def sum_squares(name, src, nk, ready):
            pe.wait_ge(*ready)
            b = begin(name)
            for k in range(nk):
                last = nc.tensor.matmul(b[:, 0:T], ones, src[:, k, :], start=(k == 0), stop=(k == nk - 1))
            done(last)

        def attention(tag, hd, nth):
            for i in range(8):
                t, grp = divmod(i, 4)
                b = begin(f"{tag}qT{i}")
                pe.wait_ge(qk_ready, 2 * nth + 2)
                qk = qk1 if hd == HD1 else qk2
                for j in range(4):
                    last = nc.tensor.transpose(b[0:hd, j * P:(j + 1) * P], qk[:, t, grp * 4 + j, :], ident)
                done(last)

            def scores(h):
                b = begin(f"{tag}S{h}")
                q, k = qkT[0:hd, h, :], qkT[0:hd, HEADS + h, :]
                nc.tensor.matmul(b[:, 0:P], q[:, 0:P], k[:, 0:P], start=True, stop=True)
                done(nc.tensor.matmul(b[:, P:P + T], q[:, P:T], k, start=True, stop=True))

            wait_emptied(pe, f"{tag}qT6")
            wait_emptied(pe, f"{tag}qT7")
            scores(0)
            for h in range(HEADS):
                if h + 1 < HEADS:
                    scores(h + 1)
                b = begin(f"{tag}PT{h}")
                pe.wait_ge(exp_ready, 2 * (HEADS * nth + h + 1))
                for q in range(3):
                    last = nc.tensor.transpose(b[:, q * P:(q + 1) * P], pb[:, h % 2, q * P:(q + 1) * P], ident)
                done(last)
                if h % 4 == 3:
                    b = begin(f"{tag}O{h // 4}")
                    wait_emptied(pe, f"{tag}PT{h}")
                    for j in range(4):
                        hh = h - 3 + j
                        pt = ptb[:, hh % 4, :]
                        vh = [vv[:, t, hh * HV:(hh + 1) * HV] for t in range(TT)]
                        nc.tensor.matmul(b[:, j * HV:(j + 1) * HV], pt[:, 0:P], vh[0], start=True, stop=True)
                        o1 = b[:, T + j * HV:T + (j + 1) * HV]
                        nc.tensor.matmul(o1, pt[:, P:2 * P], vh[0], start=True, stop=False)
                        last = nc.tensor.matmul(o1, pt[:, 2 * P:3 * P], vh[1], start=False, stop=True)
                    done(last)
            wait_emptied(pe, f"{tag}O1")
            for t in range(TT):
                turn4(f"{tag}AT{t}", lambda q, t=t: att[:, t, q * P:(q + 1) * P])
            wait_emptied(pe, f"{tag}AT1")

        def second_ada(r):
            ada(f"bda{r}", "bda", r, 1)
            wait_emptied(pe, f"bda{r}")
            turn4(f"bdaT{r}", lambda q: ada_sb[:, q * P:(q + 1) * P])

        pe.wait_ge(consts_in, 48)
        sum_squares("ss1", sqx, DC, (square_ready, 1))
        pe.wait_ge(silu_ready, 2)
        ada("ada0", "ada", 0, 0)
        wait_emptied(pe, "ada0")
        turn4("adaT0", lambda q: ada_sb[:, q * P:(q + 1) * P])
        pe.wait_ge(h_ready, 8)
        w = slab3(8, A0)(slab("in_small"))
        feature_pair("cq", w, 0, hT, DC)
        b = begin("ckr")
        for k in range(DC):
            nc.tensor.matmul(b[:, 0:T], w[:, k, QC:QC + KVC], hT[:, k, :], start=(k == 0), stop=(k == DC - 1))
        for t in range(TT):
            for k in range(DC):
                last = nc.tensor.matmul(b[:, T + t * KRC:T + (t + 1) * KRC], hT[:, k, t * P:(t + 1) * P],
                                        w[:, k, QC + KVC:A0], start=(k == 0), stop=(k == DC - 1))
        done(last)
        for i in range(4):
            feature_pair(f"lx{i}", slab3(8, 512)(slab(f"in_lx{i // 2}")), T * (i % 2), hT, DC)
        b = begin("sscq")
        pe.wait_ge(lora_sq, 1)
        nc.tensor.matmul(b[:, 0:T], ones, lsq[:, 0, :], start=True, stop=False)
        nc.tensor.matmul(b[:, 0:T], ones, lsq[:, 1, :], start=False, stop=True)
        done(nc.tensor.matmul(b[:, T:2 * T], ones, lsq[:, 2, :], start=True, stop=True))
        pe.wait_ge(lora_ready, 1)
        s = slab("qkv")
        wq = slab3(2, 768)(s)
        for t in range(TT):
            for i in range(2):
                b = begin(f"qp{t}{i}")
                for k in range(2):
                    last = nc.tensor.matmul(b[:, 0:384], cq[:, k, t * P:(t + 1) * P], wq[:, k, i * 384:(i + 1) * 384],
                                            start=(k == 0), stop=(k == 1))
                done(last)
        for t in range(TT):
            for i in range(2):
                b = begin(f"kv{t}{i}")
                done(nc.tensor.matmul(b[:, :], ckv[:, t * P:(t + 1) * P], s[:, 1536 + i * 512:2048 + i * 512],
                                      start=True, stop=True))
        for i in range(4):
            feature_pair(f"lg{i}", slab3(8, 512)(slab(f"in_lg{i // 2}")), T * (i % 2), hT, DC)
        for r in (1, 2):
            ada(f"ada{r}", "ada", r, 0)
            wait_emptied(pe, f"ada{r}")
            turn4(f"adaT{r}", lambda q: ada_sb[:, q * P:(q + 1) * P])
        s = slab("gates")
        for c in range(DC):
            b = begin(f"lr{c}")
            pe.wait_ge(conv_ready, c + 1)
            for j in range(2):
                last = nc.tensor.matmul(b[:, j * T:(j + 1) * T], s[:, 1024 * j + P * c:1024 * j + P * (c + 1)],
                                        xc[:, c, :], start=True, stop=True)
            done(last)
        for i in range(8):
            feature_pair(f"mg{i}", slab3(8, 512)(slab(f"in_mg{i // 2}")), T * (i % 2), hT, DC)
            if i % 4 == 3:
                second_ada(i // 4)
        attention("a", HD1, 0)
        second_ada(2)
        w = slab3(4, 1024)(slab("o_attn"))
        for i in range(4):
            feature_pair(f"ya{i}", w, T * i, attT, 4)
        pe.wait_ge(rec_ready, 1)
        for i in range(4):
            feature_pair(f"yl{i}", slab3(8, 512)(slab(f"o_lru{i // 2}")), T * (i % 2), gate, DC)
        pe.wait_ge(y_ready, 1)
        for i in range(4):
            feature_pair(f"xo{i}", slab3(8, 512)(slab(f"w_out{i // 2}")), T * (i % 2), yT, DC)

        sum_squares("ss2", sqx, DC, (square_ready, 2))
        pe.wait_ge(h_ready, 16)
        for i in range(8):
            feature_pair(f"pq{i}", slab3(8, 512)(slab(f"w_query{i // 2}")), T * (i % 2), hT, DC)
        keys = slab3(16, P)(slab("keys"))
        wait_emptied(pe, "pq7")
        for t in range(TT):
            for i in range(4):
                b = begin(f"sc{t}{i}")
                for j in range(4):
                    last = nc.tensor.matmul(b[:, j * P:(j + 1) * P], qT[:, 4 * i + j, t * P:(t + 1) * P],
                                            keys[:, 4 * i + j, :], start=True, stop=True)
                done(last)
        for i in range(4):
            t, half = divmod(i, 2)
            turn4(f"ht{i}", lambda q, t=t, half=half: hT[:, 4 * half + q, t * P:(t + 1) * P])

        for n in range(INDEX["ht3"] - 7, INDEX["ht3"] + 1):
            wait_emptied(pe, PLAN[n][0])
        pe.wait_ge(zero_ready, 1)
        for t in range(TT):
            banks = [ps[2 * t], ps[2 * t + 1]]
            for h in range(2):
                nc.tensor.matmul(banks[h][:, :], zero, cst[:, 0:512], start=True, stop=False)
            with pe.Fori(0, PH) as i:
                m = i + PH * t
                for grp in range(2):
                    for j, k in enumerate(V_TENSOR):
                        pe.wait_ge(diag_ready, (m * 2 + grp) * len(V_TENSOR) + (j + 1))
                        pe.wait_ge(row_in[k], (m * 4 + (2 + grp)) * 16 + 16)
                        nc.tensor.matmul(banks[0][:, :], diag[:, j, :], rows[:, k, 0:512], start=False, stop=False)
                        nc.tensor.matmul(banks[1][:, :], diag[:, j, :], rows[:, k, 512:D], start=False, stop=False)\
                            .then_inc(row_free[k], 1)
            for h in range(2):
                last = nc.tensor.matmul(banks[h][:, :], zero, cst[:, 0:512], start=False, stop=True)
            last.then_inc(sum_ready, 1)
        pe.wait_ge(peer_out, TT)
        for t in range(TT):
            for i in range(2):
                turn4(f"po{t}{i}", lambda q, t=t, i=i: peer[:, t, (4 * i + q) * P:(4 * i + q + 1) * P])

        sum_squares("ss3", sqx, DC, (square_ready, 3))
        pe.wait_ge(h_ready, 24)

        def token_tile(name, slab_name, t):
            w = slab3(8, 512)(slab(slab_name))
            b = begin(name)
            for k in range(DC):
                last = nc.tensor.matmul(b[:, :], hT[:, k, t * P:(t + 1) * P], w[:, k, :], start=(k == 0), stop=(k == DC - 1))
            done(last)

        for n, kind in enumerate(("zq", "zk", "zv")):
            for t in range(TT):
                token_tile(f"{kind}{t}", f"in2_{n}", t)
        for n, kind in enumerate(("zx", "zb", "zc")):
            for i in range(2):
                feature_pair(f"{kind}{i}", slab3(8, 512)(slab(f"in2_{3 + n}")), T * i, hT, DC)
        for i in range(8):
            feature_pair(f"zg{i}", slab3(8, 512)(slab(f"in2_{6 + i // 2}")), T * (i % 2), hT, DC)
        attention("b", HD2, 1)
        w = slab3(4, 1024)(slab("w_pa"))
        for i in range(4):
            feature_pair(f"wa{i}", w, T * i, attT, 4)
        pe.wait_ge(rec_ready, 2)
        w = slab3(4, 1024)(slab("w_pb"))
        for i in range(4):
            feature_pair(f"wb{i}", w, T * i, zb, 4)
        pe.wait_ge(y_ready, 2)
        for i in range(4):
            feature_pair(f"xp{i}", slab3(8, 512)(slab(f"w_o_2{i // 2}")), T * (i % 2), yT, DC)

        sum_squares("ss4", sqx, DC, (square_ready, 4))
        pe.wait_ge(h_ready, 32)
        for t in range(TT):
            b = begin(f"rt{t}")
            for k in range(DC):
                last = nc.tensor.matmul(b[:, 0:36], hT[:, k, t * P:(t + 1) * P], wroute[:, k, :], start=(k == 0), stop=(k == DC - 1))
            done(last)
        pe.wait_ge(assign_ready, 1)
        b = begin("cnt")
        nc.tensor.matmul(b[:, 0:32], ones, assign[:, 0, :], start=True, stop=False)
        done(nc.tensor.matmul(b[:, 0:32], ones, assign[:, 1, :], start=False, stop=True))
        b = begin("pos")
        before = K("before")
        nc.tensor.matmul(b[:, 0:32], before, assign[:, 0, :], start=True, stop=True)
        nc.tensor.matmul(b[:, 32:64], before, assign[:, 1, :], start=True, stop=False)
        done(nc.tensor.matmul(b[:, 32:64], ones, assign[:, 0, :], start=False, stop=True))
        for i in range(4):
            t, half = divmod(i, 2)
            turn4(f"hu{i}", lambda q, t=t, half=half: hT[:, 4 * half + q, t * P:(t + 1) * P])

        for n in range(len(PLAN) - 8, len(PLAN)):
            wait_emptied(pe, PLAN[n][0])
        for c in range(4):
            nc.tensor.matmul(ps[c][:, :], zero, cst[:, 0:512], start=True, stop=False)
        A, B, Cb, Db = ps[4], ps[5], ps[6], ps[7]
        fold = K("fold")

        def pick_tokens(par):
            for half in range(2):
                for t in range(TT):
                    j = 2 * half + t
                    last = nc.tensor.matmul(B[32 * j:32 * j + 32, :], pick[:, par, t, :], htok[:, t, half * 512:(half + 1) * 512],
                                            start=True, stop=True, tile_position=(0, 32 * j))
            last.then_inc(m_x4, 1)

        def fold_x():
            for c in range(4):
                last = nc.tensor.matmul(Db[:, T + 64 * c:T + 64 * c + 64], x4s[:, c * P:(c + 1) * P], fold, start=True, stop=True)
            last.then_inc(m_xt, 1)

        def combine(par):
            for c in range(DC):
                last = nc.tensor.matmul(ps[c // 2][:, (c % 2) * T:(c % 2 + 1) * T], y4s[:, par, c * P:(c + 1) * P],
                                        placeT[:, par, :], start=False, stop=False)
            last.then_inc(m_comb, 1)

        pe.wait_ge(pick_ready, 1)
        pick_tokens(0)
        pe.wait_ge(x4_out, 1)
        fold_x()
        pe.wait_ge(table_ready, 1)
        npair = pe.value_load(npair_sb[0:1, :], min_val=NEXP // 2, max_val=(NEXP + OVER) // 2)
        slot_base = [slab_value[[n for n in range(len(SL)) if n % NSLOT == q][-1]] - 16 for q in range(NSLOT)]
        with pe.Fori(0, npair) as i:
            for par in range(2):
                n1 = i * 2 + (par + 1)
                s1, s3, s2 = [(MOE0 + 3 * par + q) % NSLOT for q in range(3)]
                ws = [slab3(8, 512)(slabs[:, s1, :]), slab3(8, 512)(slabs[:, s3, :])]
                pe.wait_ge(xt_out, n1)
                pe.wait_ge(y0_out, n1)
                pe.wait_ge(slab_loaded[s1], i * 16 + slot_base[s1] + 16)
                pe.wait_ge(slab_loaded[s3], i * 16 + slot_base[s3] + 16)
                for q in range(4):
                    for j in range(4):
                        kc = 2 * q + j % 2
                        last = nc.tensor.matmul(A[32 * j:32 * j + 32, :], xts[:, par, kc % 4, kc // 4, :], ws[j // 2][:, kc, :],
                                                start=(q == 0), stop=(q == 3), tile_position=(0, 32 * j))
                last.then_inc(m_w13, 1)
                pe.wait_ge(pick_ready, n1 + 1)
                pe.wait_ge(y1_out, n1)
                pick_tokens(1 - par)
                pe.wait_ge(placeT_out, n1)
                combine(1 - par)
                pe.wait_ge(hp_out, n1)
                pe.wait_ge(hid_ready, n1)
                for c in range(4):
                    last = nc.tensor.matmul(Cb[:, 64 * c:64 * c + 64], hps[:, c * P:(c + 1) * P], fold, start=True, stop=True)
                last.then_inc(m_fold, 1)
                pe.wait_ge(place_ready, n1)
                for t in range(TT):
                    last = nc.tensor.transpose(Db[:, t * P:(t + 1) * P], place[:, t, :], ident)
                last.then_inc(m_pwt, 1)
                pe.wait_ge(x4_out, n1 + 1)
                fold_x()
                pe.wait_ge(hid_ready, n1 + 1)
                pe.wait_ge(slab_loaded[s2], i * 16 + slot_base[s2] + 16)
                w2 = slab3(4, 1024)(slabs[:, s2, :])
                for half, bk in enumerate((A, B)):
                    for j in range(4):
                        last = nc.tensor.matmul(bk[32 * j:32 * j + 32, :], hts[:, j, :], w2[:, j, half * 512:(half + 1) * 512],
                                                start=True, stop=True, tile_position=(0, 32 * j))
                    last.then_inc(m_w2, 1)
        pe.wait_ge(y0_out, npair * 2 + 1)
        pe.wait_ge(y1_out, npair * 2 + 1)
        pe.wait_ge(placeT_out, npair * 2 + 1)
        combine(1)
        for c in range(4):
            last = nc.tensor.matmul(ps[c][:, :], zero, cst[:, 0:512], start=False, stop=True)
        last.then_inc(m_comb, 1)

    @block.scalar
    def _(act):
        A = nc.scalar.activation

        def take(name):
            act.wait_ge(chunk_ready, INDEX[name] + 1)
            return bank(name)

        def freed(ins):
            ins.then_inc(emptied["A"], 1)

        steps = [0]

        def link(ins):
            steps[0] += 1
            ins.then_inc(act_step, 1)
            act.wait_ge(act_step, steps[0])

        def root(n, width):
            act.wait_ge(var_ready, n)
            A(std[:, 0:width], var[:, 0:width], ACT.Sqrt).then_inc(std_ready, 1)

        def modulated(n):
            shift = mod[:, n // 2, 24 * (n % 2):24 * (n % 2) + DC]
            for c in range(DC):
                act.wait_ge(scaled_ready, DC * n + c + 1)
                A(hT[:, c, :], hT[:, c, :], ACT.Identity, bias=shift[:, c:c + 1]).then_inc(h_ready, 1)

        def ada_out(name):
            if name != "ada0":
                prev = {"ada1": "adaT0", "ada2": "adaT1", "bda0": "adaT2", "bda1": "bdaT0", "bda2": "bdaT1"}[name]
                act.wait_ge(chunk_ready, INDEX[prev] + 1)
            freed(A(ada_sb[:, :], take(name)[:, :], ACT.Copy))

        def second_ada_out(r):
            ada_out(f"bda{r}")
            b = take(f"bdaT{r}")
            freed(A(mod[:, 1, 16 * r:16 * r + 16].rearrange("p (j q) -> p q j", j=4),
                    b[:, :].rearrange("p (q j x) -> p q j x", q=4, j=4)[:, :, :, 0], ACT.Copy))

        def attention(tag, hd, nth):
            qk = qk1 if hd == HD1 else qk2
            sq = sq1 if hd == HD1 else sq2
            for t in range(TT):
                act.wait_ge(qk_in, 2 * nth + t + 1)
                A(sq[:, :, :], qk[:, t, :, :], ACT.Square).then_inc(qk_square, 1)
                root(NORMS[f"{tag}qk{t}"], 16)

        def attention_rest(tag, hd, nth):
            scale = hd ** -0.5
            for i in range(1, 8, 2):
                t, grp = divmod(i, 4)
                b = take(f"{tag}qT{i}")
                freed(A(qkT[0:hd, grp * 4:grp * 4 + 4, t * P:(t + 1) * P],
                        b[0:hd, :].rearrange("p (h t) -> p h t", h=4), ACT.Copy))
            for h in range(HEADS):
                m = HEADS * nth + h
                act.wait_ge(bias_ready, m + 1)
                if h >= 2:
                    act.wait_ge(chunk_ready, INDEX[f"{tag}PT{h - 2}"] + 1)
                for t, (a, z) in enumerate(((0, P), (P, 3 * P))):
                    A(pb[:, h % 2, a:z], sm[:, h % 2, a:z], ACT.Exp, bias=nmax[:, h, t:t + 1], scale=scale,
                      accum_out=rsum[:, t, h:h + 1]).then_inc(exp_ready, 1)
                if h >= 1:
                    freed(A(ptb[:, (h - 1) % 4, :], take(f"{tag}PT{h - 1}")[:, 0:3 * P], ACT.Copy))
            freed(A(ptb[:, 3, :], take(f"{tag}PT7")[:, 0:3 * P], ACT.Copy))
            for t in range(TT):
                b = take(f"{tag}AT{t}")
                freed(A(attT[:, :, t * P:(t + 1) * P], b[:, :].rearrange("p (c t) -> p c t", c=4), ACT.Copy))

        act.wait_ge(inputs_in, 48)
        A(sqx[:, :, :], xT[:, :, :], ACT.Square).then_inc(square_ready, 1)
        for n, name in enumerate(("c", "c_2")):
            A(csb[:, n, :, :], C(name).unsqueeze(2).to_broadcast([P, DC, 32]), ACT.Silu).then_inc(silu_ready, 1)
        act.wait_ge(trig_arg, 1)
        A(trig[:, 4, :], trig[:, 2, :], ACT.Sin).then_inc(trig_done, 1)
        A(trig[:, 5, :], trig[:, 3, :], ACT.Sin).then_inc(trig_done, 1)
        act.wait_ge(lru_const, 1)
        A(small[:, 2, :], small[:, 1, :], ACT.Exp).then_inc(lam_exp, 1)
        root(1, T)
        ada_out("ada0")
        modulated(0)
        root(NORMS["lora"], 512)
        for t in range(TT):
            for i in range(2):
                b = take(f"qp{t}{i}")
                freed(A(qk1[:, t, 4 * i:4 * i + 4, :], b[:, 0:384].rearrange("p (h d) -> p h d", h=4), ACT.Copy))
        attention("a", HD1, 0)
        for i in range(4):
            freed(A(gate[:, 2 * i:2 * i + 2, :], take(f"lg{i}")[:, :].rearrange("p (c t) -> p c t", c=2), ACT.Gelu_apprx_tanh))
        for r in (1, 2):
            ada_out(f"ada{r}")
        act.wait_ge(lru_const, 2)
        for c in range(DC + 1):
            if c < DC:
                b = take(f"lr{c}")
                if c >= 2:
                    act.wait_ge(input_scale, c - 1)
                    act.wait_ge(decay_ready, 2 * (c - 1))
                A(gexp[:, c % 2, 0:T], b[:, 0:T], ACT.Exp, bias=small[:, 8, c:c + 1], scale=-1.0)
                freed(A(gexp[:, c % 2, T:2 * T], b[:, T:2 * T], ACT.Exp, bias=small[:, 9, c:c + 1], scale=-1.0))
            if c >= 1:
                d = c - 1
                act.wait_ge(gate_val, d + 1)
                if d >= 2:
                    act.wait_ge(decay_sq, d - 1)
                A(dec[:, d, :], gexp[:, d % 2, 0:T], ACT.Exp, scale=small[:, 7, d:d + 1]).then_inc(decay_ready, 1)
                A(gth[:, d % 2, :], gexp[:, d % 2, 0:T], ACT.Tanh, scale=small[:, 6, d:d + 1]).then_inc(decay_ready, 1)
        act.wait_ge(decay_sq, DC)
        A(lxm[:, :, :], lxm[:, :, :], ACT.Sqrt).then_inc(lru_root, 1)
        for i in range(8):
            freed(A(merge[:, 2 * i:2 * i + 2, :], take(f"mg{i}")[:, :].rearrange("p (c t) -> p c t", c=2), ACT.Sigmoid))
            if i % 4 == 3:
                second_ada_out(i // 4)
        act.wait_ge(rec_ready, 1)
        attention_rest("a", HD1, 0)
        second_ada_out(2)
        act.wait_ge(x_ready, 1)
        A(sqx[:, :, :], xT[:, :, :], ACT.Square).then_inc(square_ready, 1)
        root(NORMS["n2"], T)
        modulated(1)
        for i in range(8):
            freed(A(qT[:, 2 * i:2 * i + 2, :], take(f"pq{i}")[:, :].rearrange("p (c t) -> p c t", c=2), ACT.Copy))
        for t in range(TT):
            for i in (0, 2):
                freed(A(sc[:, t, i * 512:(i + 1) * 512], take(f"sc{t}{i}")[:, :], ACT.Copy))
        for i in range(4):
            freed(A(htok[:, i // 2, (i % 2) * 512:(i % 2 + 1) * 512], take(f"ht{i}")[:, :], ACT.Copy))
        for t in range(TT):
            with act.Fori(0, PH // 2) as i:
                for par in range(2):
                    m = i * 2 + (PH * t + par)
                    act.wait_ge(best_ready, m + 1)
                    A(gsoft[:, par, :], gsoft[:, par, :], ACT.Exp, accum_out=gsum[:, par, 0:1]).then_inc(best_exp, 1)
                    act.wait_ge(row_free[NROW - 1], m * 4 + 3)
                    A(wexp[:, par, :], dots[:, par, :], ACT.Gelu_apprx_tanh).then_inc(gelu_ready, 1)
                    act.wait_ge(weight_ready, m + 1)
                    for grp in range(2):
                        for j, k in enumerate(V_TENSOR):
                            act.wait_ge(row_free[k], m * 4 + (1 + 3 * grp))
                            A(diag[:, j, :], ident, ACT.Copy, scale=wexp[:, par, grp * NROW + k:grp * NROW + k + 1]).then_inc(diag_ready, 1)

        act.wait_ge(x_ready, 2)
        A(sqx[:, :, :], xT[:, :, :], ACT.Square).then_inc(square_ready, 1)
        root(NORMS["n3"], T)
        modulated(2)
        for t in range(TT):
            freed(A(qk2[:, t, 0:8, :], take(f"zq{t}")[:, :].rearrange("p (h d) -> p h d", h=8), ACT.Copy))
        for t in range(TT):
            freed(A(vv[:, t, :], take(f"zv{t}")[:, :], ACT.Copy))
        attention("b", HD2, 1)
        for dst, kind in ((zx, "zx"), (zb, "zb")):
            for i in range(2):
                freed(A(dst[:, 2 * i:2 * i + 2, :], take(f"{kind}{i}")[:, :].rearrange("p (c t) -> p c t", c=2), ACT.Copy))
        for i in range(8):
            freed(A(merge[:, 2 * i:2 * i + 2, :], take(f"zg{i}")[:, :].rearrange("p (c t) -> p c t", c=2), ACT.Sigmoid))
        act.wait_ge(rec_ready, 2)
        attention_rest("b", HD2, 1)
        act.wait_ge(x_ready, 3)
        A(sqx[:, :, :], xT[:, :, :], ACT.Square).then_inc(square_ready, 1)
        root(NORMS["n4"], T)
        modulated(3)
        act.wait_ge(routed_ready, 1)
        A(gexp4[:, :, :], logit[:, :, 0:4], ACT.Exp).then_inc(route_exp, 1)
        act.wait_ge(routed_ready, 2)
        A(gate2v[:, :, 1:2], gate2v[:, :, 0:1], ACT.Exp).then_inc(route_exp, 1)
        for i in range(4):
            freed(A(htok[:, i // 2, (i % 2) * 512:(i % 2 + 1) * 512], take(f"hu{i}")[:, :], ACT.Copy))
        act.wait_ge(m_xt, 1)
        A(xts[:, 0, :, :, :], ps[7][:, T:2 * T].rearrange("p (c a s) -> p c a s", c=4, a=2), ACT.Copy).then_inc(xt_out, 1)
        act.wait_ge(table_ready, 1)
        npair = act.value_load(npair_sb[0:1, :], min_val=NEXP // 2, max_val=(NEXP + OVER) // 2)
        with act.Fori(0, npair) as i:
            for par in range(2):
                n1 = i * 2 + (par + 1)
                act.wait_ge(m_w13, n1)
                A(hps[:, :], ps[4][:, :], ACT.Copy).then_inc(hp_out, 1)
                act.wait_ge(m_fold, n1)
                act.wait_ge(hid_ready, n1)
                A(sil[:, :, :], ps[6][:, 0:T].rearrange("p (c a s) -> p c a s", c=4, a=2)[:, :, 0, :], ACT.Silu)\
                    .then_inc(silu_out, 1)
                act.wait_ge(m_xt, n1 + 1)
                A(xts[:, 1 - par, :, :, :], ps[7][:, T:2 * T].rearrange("p (c a s) -> p c a s", c=4, a=2), ACT.Copy)\
                    .then_inc(xt_out, 1)
                A(placeT[:, par, :], ps[7][:, 0:T], ACT.Copy).then_inc(placeT_out, 1)
                act.wait_ge(m_w2, n1 * 2 - 1)
                A(y4s[:, par, 0:512], ps[4][:, :], ACT.Copy).then_inc(y0_out, 1)

    @block.gpsimd
    def _(pool):
        nc.gpsimd.memset(tick0[:, :], 0).then_inc(pool_tick, 1)
        pool.wait_ge(pool_tick, 1)
        for t in range(TT):
            with pool.Fori(0, PH // 2) as i:
                for par in range(2):
                    m = i * 2 + (PH * t + par)
                    pool.wait_ge(index_ready, m + 1)
                    nc.gpsimd.tensor_tensor(idx_stage[:, par, :], eidx[:, par, :], tick0[:, :].to_broadcast([P, TOPK]), ALU.add)\
                        .then_inc(index_staged, 1)
                    pool.wait_ge(index_staged, m + 1)
                    for grp in range(4):
                        for k in range(NROW):
                            pool.wait_ge(pool_tick, m * 32 + (grp * NROW + k + 1))
                            pool.wait_ge(row_free[k], m * 4 + (grp + 1))
                            nc.gpsimd.tensor_tensor(tick[:, :], tick0[:, :], tick0[:, :], ALU.add).then_inc(pool_tick, 1)
                            n = (grp % 2) * NROW + k
                            nc.gpsimd.indirect_dma_start(
                                out=rows[:, k, :], out_offset=None, in_=g["expert_u" if grp < 2 else "expert_v"],
                                in_offset=bass.IndirectOffsetOnAxis(ap=idx_stage[:, par, n:n + 1], axis=0))\
                                .then_inc(row_in[k], 16)

    @block.vector
    def _(dve):
        V = nc.vector
        steps = [0]

        def link(ins):
            steps[0] += 1
            ins.then_inc(dve_step, 1)
            dve.wait_ge(dve_step, steps[0])

        def take(name):
            dve.wait_ge(chunk_ready, INDEX[name] + 1)
            return bank(name)

        def freed(name, ins):
            ins.then_inc(emptied["D"], 1)
            dve.wait_ge(emptied["D"], evacs("D", INDEX[name]))

        def pair(b, n=2):
            return b[:, :].rearrange("p (c t) -> p c t", c=n)

        def inverse_root(n, width):
            v, s, r, w = var[:, 0:width], std[:, 0:width], rst[:, 0:width], newt[:, 0:width]
            dve.wait_ge(std_ready, n)
            link(V.reciprocal(r, s))
            link(V.tensor_tensor(w, r, r, ALU.mult))
            link(V.tensor_tensor(w, w, v, ALU.mult))
            link(V.tensor_scalar(w, w, -0.5, 1.5, ALU.mult, ALU.add))
            link(V.tensor_tensor(r, r, w, ALU.mult))

        def stream_norm(n, name, norm):
            b = take(name)
            freed(name, V.tensor_scalar(var[:, 0:T], b[:, 0:T], 1.0 / D, EPS, ALU.mult, ALU.add))
            V.nop().then_inc(var_ready, 1)
            inverse_root(NORMS[norm], T)

        def scaled(n):
            for c in range(DC):
                V.scalar_tensor_tensor(out=hT[:, c, :], in0=xT[:, c, :], scalar=amul[:, n, c:c + 1], in1=rst[:, 0:T],
                                       op0=ALU.mult, op1=ALU.mult).then_inc(scaled_ready, 1)
            dve.wait_ge(h_ready, DC * (n + 1))

        def amuls(n, gname):
            b, k = divmod(n, 2)
            link(V.scalar_tensor_tensor(out=amul[:, n, :], in0=mod[:, b, 24 * k + 8:24 * k + 16], scalar=1.0, in1=C(gname),
                                        op0=ALU.add, op1=ALU.mult))

        def ada_columns(name, r):
            b = take(name)
            a0 = COL["b_ada"][0] + 16 * r
            freed(name, V.tensor_tensor(mod[:, 0, 16 * r:16 * r + 16].rearrange("p (j q) -> p q j", j=4),
                                        b[:, :].rearrange("p (q j x) -> p q j x", q=4, j=4)[:, :, :, 0],
                                        cols[:, a0:a0 + 16].rearrange("p (j q) -> p q j", j=4), ALU.add))

        def qk_norm(tag, hd, nth, t, r0, half, cos, sin, gq, gk):
            qk = (qk1 if hd == HD1 else qk2)[:, t, :, :]
            sq = sq1 if hd == HD1 else sq2
            dve.wait_ge(qk_square, 2 * nth + t + 1)
            link(V.tensor_reduce(out=var[:, 0:16], in_=sq[:, :, :], axis=AX.X, op=ALU.add))
            link(V.tensor_scalar(var[:, 0:16], var[:, 0:16], 1.0 / hd, EPS, ALU.mult, ALU.add))
            V.nop().then_inc(var_ready, 1)
            inverse_root(NORMS[f"{tag}qk{t}"], 16)
            link(V.tensor_tensor(qk, qk, rst[:, 0:16].unsqueeze(2).to_broadcast([P, 16, hd]), ALU.mult))
            V.tensor_tensor(qk[:, 0:8, :], qk[:, 0:8, :], gq.unsqueeze(1).to_broadcast([P, 8, hd]), ALU.mult)
            link(V.tensor_tensor(qk[:, 8:16, :], qk[:, 8:16, :], gk.unsqueeze(1).to_broadcast([P, 8, hd]), ALU.mult))
            t1, t2 = qk[:, :, r0:r0 + half], qk[:, :, r0 + half:r0 + 2 * half]
            cb = cos.unsqueeze(1).to_broadcast([P, 16, half])
            sb_ = sin.unsqueeze(1).to_broadcast([P, 16, half])
            rt = [r[:, 0:16 * half].rearrange("p (h d) -> p h d", h=16) for r in rot]
            V.tensor_tensor(rt[0], t1, cb, ALU.mult)
            V.tensor_tensor(rt[1], t2, sb_, ALU.mult)
            V.tensor_tensor(rt[2], t1, sb_, ALU.mult)
            link(V.tensor_tensor(rt[3], t2, cb, ALU.mult))
            V.tensor_tensor(t1, rt[0], rt[1], ALU.subtract)
            link(V.tensor_tensor(t2, rt[2], rt[3], ALU.add))
            V.nop().then_inc(qk_ready, 1)

        def attention(tag, hd, nth, bound):
            scale = hd ** -0.5
            for i in range(0, 8, 2):
                t, grp = divmod(i, 4)
                b = take(f"{tag}qT{i}")
                freed(f"{tag}qT{i}", V.tensor_copy(qkT[0:hd, grp * 4:grp * 4 + 4, t * P:(t + 1) * P],
                                                   b[0:hd, :].rearrange("p (h t) -> p h t", h=4)))
            for h in range(HEADS):
                m = HEADS * nth + h
                s = sm[:, h % 2, :]
                if h >= 2:
                    dve.wait_ge(exp_ready, 2 * (m - 1))
                freed(f"{tag}S{h}", V.tensor_tensor(s, take(f"{tag}S{h}")[:, 0:3 * P], bound, ALU.min))
                V.tensor_reduce(out=nmax[:, h, 0:1], in_=s[:, 0:P], axis=AX.X, op=ALU.max)
                link(V.tensor_reduce(out=nmax[:, h, 1:2], in_=s[:, P:3 * P], axis=AX.X, op=ALU.max))
                V.tensor_scalar(nmax[:, h, :], nmax[:, h, :], -scale, None, ALU.mult).then_inc(bias_ready, 1)
                if h in (4, 7):
                    grp = 0 if h == 4 else 1
                    if h == 4:
                        heads_out(tag, nth, 0)
            heads_out(tag, nth, 1)

        def heads_out(tag, nth, grp):
            dve.wait_ge(exp_ready, 2 * (HEADS * nth + 4 * grp + 4))
            link(V.reciprocal(rinv[:, :, 4 * grp:4 * grp + 4], rsum[:, :, 4 * grp:4 * grp + 4]))
            b = take(f"{tag}O{grp}")
            freed(f"{tag}O{grp}", V.tensor_tensor(
                att[:, :, T * grp:T * (grp + 1)].rearrange("p t (h d) -> p t h d", h=4),
                b[:, :].rearrange("p (t h d) -> p t h d", t=TT, h=4),
                rinv[:, :, 4 * grp:4 * grp + 4].unsqueeze(3).to_broadcast([P, TT, 4, HV]), ALU.mult))

        def merged(first, second, nth):
            for i in range(4):
                freed(f"{first}{i}", V.tensor_tensor(yT[:, 2 * i:2 * i + 2, :], pair(take(f"{first}{i}")),
                                                     merge[:, 2 * i:2 * i + 2, :], ALU.mult))
            for i in range(4):
                tmp = ytmp[:, i % 2, :].rearrange("p (c t) -> p c t", c=2)
                freed(f"{second}{i}", V.tensor_tensor(tmp, pair(take(f"{second}{i}")),
                                                      merge[:, 8 + 2 * i:10 + 2 * i, :], ALU.mult))
                link(V.tensor_tensor(yT[:, 2 * i:2 * i + 2, :], yT[:, 2 * i:2 * i + 2, :], tmp, ALU.add))
            V.nop().then_inc(y_ready, 1)

        def residual(name, b):
            for i in range(4):
                bk = take(f"{name}{i}")
                for q in range(2):
                    c = 2 * i + q
                    ins = V.scalar_tensor_tensor(out=xT[:, c, :], in0=bk[:, q * T:(q + 1) * T], scalar=mod[:, b, 16 + c:17 + c],
                                                 in1=xT[:, c, :], op0=ALU.mult, op1=ALU.add)
                freed(f"{name}{i}", ins)

        V.memset(zero, 0.0).then_inc(zero_ready, 1)
        V.memset(lx[:, :, 0:3], 0.0)
        for k in range(NROW):
            V.nop().then_inc(row_free[k], 1)
        dve.wait_ge(inputs_in, 48)
        dve.wait_ge(consts_in, 48)
        lam = C("lru_lambda")
        link(V.tensor_scalar(small[:, 10, :], lam, -1.0, None, ALU.mult))
        link(V.tensor_tensor(small[:, 1, :], lam, small[:, 10, :], ALU.min))
        V.tensor_scalar(small[:, 8, :], C("b_rg"), -1.0, None, ALU.mult)
        V.tensor_scalar(small[:, 9, :], C("b_ig"), -1.0, None, ALU.mult).then_inc(lru_const, 1)
        ang, turns, red, quarter = trig[:, 0, :], trig[:, 1, :], trig[:, 2, :], trig[:, 3, :]
        link(V.tensor_copy(posf[:, :], posn[:, :]))
        for t in range(TT):
            link(V.tensor_scalar(ang[:, 16 * t:16 * t + 16], K("freq"), posf[:, t:t + 1], None, ALU.mult))
        MAGIC = 12582912.0
        link(V.tensor_scalar(turns, ang, 1.0 / (2 * math.pi), None, ALU.mult))
        link(V.tensor_scalar(turns, turns, MAGIC, None, ALU.add))
        link(V.tensor_scalar(turns, turns, -MAGIC, None, ALU.add))
        rest = 2 * math.pi
        src = ang
        for bits in (8, 11, 24):
            part = float(np.round(rest * 2.0 ** (bits - 3)) / 2.0 ** (bits - 3)) if bits < 24 else float(np.float32(rest))
            if bits == 11:
                part = float(np.round(rest * 2.0 ** 16) / 2.0 ** 16)
            rest -= part
            link(V.scalar_tensor_tensor(out=red, in0=turns, scalar=-part, in1=src, op0=ALU.mult, op1=ALU.add))
            src = red
        link(V.tensor_scalar(red, red, 3.1415925, -3.1415925, ALU.min, ALU.max))
        link(V.tensor_scalar(quarter, red, -1.0, None, ALU.mult))
        link(V.tensor_tensor(quarter, quarter, red, ALU.max))
        link(V.tensor_scalar(quarter, quarter, -1.0, math.pi / 2, ALU.mult, ALU.add))
        V.nop().then_inc(trig_arg, 1)
        dve.wait_ge(lam_exp, 1)
        e, z, z2, q = small[:, 2, :], small[:, 3, :], small[:, 4, :], small[:, 5, :]
        link(V.tensor_scalar(q, e, 2.0, None, ALU.add))
        link(V.reciprocal(z, q))
        link(V.tensor_tensor(z, z, e, ALU.mult))
        link(V.tensor_tensor(z2, z, z, ALU.mult))
        link(V.tensor_scalar(q, z2, 1.0 / 19, None, ALU.mult))
        for n in range(8, 0, -1):
            link(V.scalar_tensor_tensor(out=q, in0=q, scalar=1.0 / (2 * n + 1), in1=z2, op0=ALU.add, op1=ALU.mult))
        link(V.scalar_tensor_tensor(out=q, in0=q, scalar=1.0, in1=z, op0=ALU.add, op1=ALU.mult))
        link(V.tensor_scalar(small[:, 10, :], small[:, 10, :], 0.0, None, ALU.max))
        link(V.scalar_tensor_tensor(out=q, in0=q, scalar=2.0, in1=small[:, 10, :], op0=ALU.mult, op1=ALU.add))
        link(V.tensor_scalar(small[:, 6, :], q, 8.0, None, ALU.mult))
        link(V.tensor_scalar(small[:, 7, :], q, -8.0, None, ALU.mult))
        V.nop().then_inc(lru_const, 1)

        stream_norm(0, "ss1", "n1")
        ada_columns("adaT0", 0)
        amuls(0, "norm1_g")
        scaled(0)
        freed("cq", V.tensor_copy(cq[:, :, :], pair(take("cq"))))
        b = take("ckr")
        V.tensor_copy(ckv, b[:, 0:T])
        freed("ckr", V.tensor_copy(krope[:, :, :], b[:, T:T + 64].rearrange("p (t r) -> p t r", t=TT)))
        link(V.tensor_tensor(lsq[:, 0:2, :], cq[:, :, :], cq[:, :, :], ALU.mult))
        V.tensor_tensor(lsq[:, 2, :], ckv, ckv, ALU.mult).then_inc(lora_sq, 1)
        for i in range(4):
            freed(f"lx{i}", V.tensor_copy(lx[:, 2 * i:2 * i + 2, 3:3 + T], pair(take(f"lx{i}"))))

        def conv(c):
            dst = xc[:, c, :]
            link(V.tensor_scalar(dst, lx[:, c, 0:T], C("conv_w", c), C("conv_b", c), ALU.mult, ALU.add))
            for j in range(1, 4):
                ins = V.scalar_tensor_tensor(out=dst, in0=lx[:, c, j:j + T], scalar=C("conv_w", 8 * j + c), in1=dst,
                                             op0=ALU.mult, op1=ALU.add)
                if j < 3:
                    link(ins)
            ins.then_inc(conv_ready, 1)

        b = take("sscq")
        V.tensor_scalar(var[:, 0:T], b[:, 0:T], 1.0 / QC, EPS, ALU.mult, ALU.add)
        freed("sscq", V.tensor_scalar(var[:, T:2 * T], b[:, T:2 * T], 1.0 / KVC, EPS, ALU.mult, ALU.add))
        V.nop().then_inc(var_ready, 1)
        for c in range(3):
            conv(c)
        inverse_root(NORMS["lora"], 512)
        for k in range(2):
            V.scalar_tensor_tensor(out=cq[:, k, :], in0=cq[:, k, :], scalar=C("q_a_norm_g", k), in1=rst[:, 0:T],
                                   op0=ALU.mult, op1=ALU.mult)
        V.scalar_tensor_tensor(out=ckv, in0=ckv, scalar=C("kv_a_norm_g", 0), in1=rst[:, T:2 * T],
                               op0=ALU.mult, op1=ALU.mult).then_inc(lora_ready, 1)
        for t in range(TT):
            for i in range(2):
                b = take(f"kv{t}{i}")[:, :].rearrange("p (h d) -> p h d", h=4)
                V.tensor_copy(qk1[:, t, 8 + 4 * i:12 + 4 * i, 0:HV], b[:, :, 0:HV])
                freed(f"kv{t}{i}", V.tensor_copy(vv[:, t, T * i:T * (i + 1)].rearrange("p (h d) -> p h d", h=4), b[:, :, HV:2 * HV]))
            wait_emptied(dve, f"qp{t}1")
            V.tensor_copy(qk1[:, t, 8:16, HV:HD1], krope[:, t, :].unsqueeze(1).to_broadcast([P, 8, KRC])).then_inc(qk_in, 1)
        for c in range(3, DC):
            conv(c)
        dve.wait_ge(trig_done, 2)
        for t in range(TT):
            qk_norm("a", HD1, 0, t, HV, 16, trig[:, 5, 16 * t:16 * t + 16], trig[:, 4, 16 * t:16 * t + 16], R("q_norm_g"), R("k_norm_g"))
        for r in (1, 2):
            ada_columns(f"adaT{r}", r)
        amuls(1, "norm2_g")
        for c in range(DC):
            gx = gexp[:, c % 2, :]
            dve.wait_ge(emptied["A"], evacs("A", INDEX[f"lr{c}"]))
            link(V.tensor_scalar(gx, gx, 1.0, None, ALU.add))
            V.reciprocal(gx, gx).then_inc(gate_val, 1)
            dve.wait_ge(gate_val, c + 1)
            V.tensor_tensor(xc[:, c, :], gx[:, T:2 * T], xc[:, c, :], ALU.mult).then_inc(input_scale, 1)
            dve.wait_ge(decay_ready, 2 * c + 2)
            link(V.tensor_tensor(ga2, dec[:, c, :], dec[:, c, :], ALU.mult))
            V.scalar_tensor_tensor(out=lxm[:, c, :], in0=ga2, scalar=1.0, in1=gth[:, c % 2, :],
                                   op0=ALU.add, op1=ALU.mult).then_inc(decay_sq, 1)
            dve.wait_ge(decay_sq, c + 1)
        dve.wait_ge(lru_root, 1)
        link(V.tensor_tensor(xc[:, :, :], xc[:, :, :], lxm[:, :, :], ALU.mult))
        for c in range(DC):
            ins = V.tensor_tensor_scan(out=xc[:, c, :], data0=dec[:, c, :], data1=xc[:, c, :], initial=0.0,
                                       op0=ALU.mult, op1=ALU.add)
        link(ins)
        wait_emptied(dve, "lg3")
        V.tensor_tensor(gate[:, :, :], gate[:, :, :], xc[:, :, :], ALU.mult).then_inc(rec_ready, 1)
        dve.wait_ge(rec_ready, 1)
        attention("a", HD1, 0, K("bound1"))
        wait_emptied(dve, "mg7")
        merged("ya", "yl", 0)
        residual("xo", 0)
        V.nop().then_inc(x_ready, 1)

        stream_norm(1, "ss2", "n2")
        scaled(1)
        for t in range(TT):
            for i in (1, 3):
                freed(f"sc{t}{i}", V.tensor_copy(sc[:, t, i * 512:(i + 1) * 512], take(f"sc{t}{i}")[:, :]))

        def route(m, par):
            n = [0]

            def then(ins, plain=False):
                n[0] += 1
                ins.then_inc(route_step, 1)
                dve.wait_ge(route_step, m * ROUTE + n[0])
                if plain:
                    V.tensor_copy(carrier, zero[:, 0:1])

            def top16(lists):
                for half in range(2):
                    a, z = 8 * half, 8 * half + 8
                    ins = [V.max(out=v[:, a:z], in_=src) for v, x, src in lists][-1]
                    then(ins, plain=True)
                    ins = [V.max_index(out=x[:, a:z], in_max=v[:, a:z], in_values=src) for v, x, src in lists][-1]
                    then(ins, plain=half == 0)
                    if half == 0:
                        ins = [V.match_replace(out=src, in_to_replace=v[:, a:z], in_values=src, imm_value=-BIG)
                               for v, x, src in lists][-1]
                        then(ins, plain=True)

            at = m * 256
            then(V.tensor_copy(stage, sc_flat[:, at:at + 256] if isinstance(m, int) else sc_flat[:, bass.ds(at, 256)]), plain=True)
            top16([(stop_[:, q, :], itop[:, q, :], stage[:, q * NKEY:(q + 1) * NKEY]) for q in range(2)])
            V.tensor_copy(itopf[:, :, :], itop[:, :, :])
            then(V.tensor_tensor(cand.rearrange("p (a b) -> p a b", a=TOPK),
                                 stop_[:, 0, :].unsqueeze(2).to_broadcast([P, TOPK, TOPK]),
                                 stop_[:, 1, :].unsqueeze(1).to_broadcast([P, TOPK, TOPK]), ALU.add), plain=True)
            top16([(best, bpos, cand)])
            V.tensor_tensor(gsoft[:, par, :], best, best[:, 0:1].to_broadcast([P, TOPK]), ALU.subtract).then_inc(best_ready, 1)
            V.tensor_single_scalar(bhalf[:, 0, :], bpos, 4, ALU.logical_shift_right)
            then(V.tensor_single_scalar(bhalf[:, 1, :], bpos, 15, ALU.bitwise_and))
            then(V.tensor_copy(bhalff[:, :, :], bhalf[:, :, :]))
            for q in range(2):
                ins = V.tensor_tensor(hot[:, q, :, :], bhalff[:, q, :].unsqueeze(2).to_broadcast([P, TOPK, TOPK]),
                                      K("iota32")[:, 0:TOPK].unsqueeze(1).to_broadcast([P, TOPK, TOPK]), ALU.is_equal)
            then(ins)
            for q in range(2):
                ins = V.tensor_tensor(hot[:, q, :, :], hot[:, q, :, :], itopf[:, q, :].unsqueeze(1).to_broadcast([P, TOPK, TOPK]), ALU.mult)
            then(ins)
            then(V.tensor_reduce(out=ihalf[:, :, :], in_=hot[:, :, :, :], axis=AX.X, op=ALU.add))
            then(V.scalar_tensor_tensor(out=ihalf[:, 0, :], in0=ihalf[:, 0, :], scalar=float(NKEY), in1=ihalf[:, 1, :],
                                        op0=ALU.mult, op1=ALU.add))
            V.tensor_copy(eidx[:, par, :], ihalf[:, 0, :]).then_inc(index_ready, 1)
            assert n[0] == ROUTE, n[0]

        def head(m, par, t, last=False):
            for grp in range(2):
                for k in range(NROW):
                    dve.wait_ge(row_in[k], (m * 4 + grp) * 16 + 16)
                    n = grp * NROW + k
                    V.tensor_tensor_reduce(out=rows[:, k, :], in0=rows[:, k, :], in1=htok[:, t, :], scale=1.0, scalar=0.0,
                                           op0=ALU.mult, op1=ALU.add, accum_out=dots[:, par, n:n + 1]).then_inc(row_free[k], 1)
            dve.wait_ge(best_exp, m + 1)
            V.reciprocal(gsum[:, par, 1:2], gsum[:, par, 0:1]).then_inc(sum_inverse, 1)
            dve.wait_ge(sum_inverse, m + 1)
            dve.wait_ge(gelu_ready, m + 1)
            V.scalar_tensor_tensor(out=wexp[:, par, :], in0=wexp[:, par, :], scalar=gsum[:, par, 1:2], in1=gsoft[:, par, :],
                                   op0=ALU.mult, op1=ALU.mult).then_inc(weight_ready, 1)
            if not last:
                route(m + 1, 1 - par)
            dve.wait_ge(weight_ready, m + 1)
            for grp in range(2):
                for j, k in enumerate(V_VECTOR):
                    dve.wait_ge(row_free[V_VECTOR[j - 1]], m * 4 + ((4 if j else 3) + grp if grp or j else 1))
                    dve.wait_ge(row_in[k], (m * 4 + (2 + grp)) * 16 + 16)
                    n = grp * NROW + k
                    V.scalar_tensor_tensor(out=accv, in0=rows[:, k, :], scalar=wexp[:, par, n:n + 1], in1=accv,
                                           op0=ALU.mult, op1=ALU.add).then_inc(row_free[k], 1)

        wait_emptied(dve, "sc12")
        wait_emptied(dve, "sc13")
        route(0, 0)
        a0 = COL["b_ada_2"][0]
        link(V.tensor_tensor(mod[:, 1, :], mod[:, 1, :], cols[:, a0:a0 + 48], ALU.add))
        amuls(2, "g_norm1_2")
        amuls(3, "g_norm2_2")
        wait_emptied(dve, "ht3")
        for t in range(TT):
            V.memset(accv, 0.0).then_inc(acc_step, 1)
            dve.wait_ge(acc_step, t + 1)
            pairs = PH // 2 - (1 if t == TT - 1 else 0)
            with dve.Fori(0, pairs) as i:
                for par in range(2):
                    head(i * 2 + (PH * t + par), par, t)
            if t == TT - 1:
                head(TT * PH - 2, 0, t)
                head(TT * PH - 1, 1, t, last=True)
            dve.wait_ge(row_free[V_VECTOR[-1]], 4 * PH * (t + 1) + 1)
            dve.wait_ge(sum_ready, t + 1)
            V.tensor_tensor(peer[:, t, 0:512], ps[2 * t][:, :], accv[:, 0:512], ALU.add)
            link(V.tensor_tensor(peer[:, t, 512:D], ps[2 * t + 1][:, :], accv[:, 512:D], ALU.add))
            V.nop().then_inc(peer_out, 1)
        for t in range(TT):
            for i in range(2):
                b = take(f"po{t}{i}")
                for q in range(4):
                    c = 4 * i + q
                    x = xT[:, c, t * P:(t + 1) * P]
                    ins = V.scalar_tensor_tensor(out=x, in0=b[:, q * P:(q + 1) * P], scalar=mod[:, 0, 40 + c:41 + c], in1=x,
                                                 op0=ALU.mult, op1=ALU.add)
                freed(f"po{t}{i}", ins)
        V.nop().then_inc(x_ready, 1)

        stream_norm(2, "ss3", "n3")
        scaled(2)
        for t in range(TT):
            freed(f"zk{t}", V.tensor_copy(qk2[:, t, 8:16, :], take(f"zk{t}")[:, :].rearrange("p (h d) -> p h d", h=8)))
            wait_emptied(dve, f"zq{t}")
            V.nop().then_inc(qk_in, 1)
        V.memset(cx[:, :, 0:2], 0.0)
        for t in range(TT):
            qk_norm("b", HD2, 1, t, 0, 8, K("cos2")[:, 8 * t:8 * t + 8], K("sin2")[:, 8 * t:8 * t + 8], R("g_q_2"), R("g_k_2"))
        wait_emptied(dve, "zx1")
        wait_emptied(dve, "zb1")
        for i in range(2):
            freed(f"zc{i}", V.tensor_tensor(cx[:, 2 * i:2 * i + 2, 2:2 + T], pair(take(f"zc{i}")), zx[:, 2 * i:2 * i + 2, :], ALU.mult))
        for c in range(4):
            link(V.tensor_scalar(cv[:, c, :], cx[:, c, 0:T], C("conv_w_2", c), C("conv_b_2", c), ALU.mult, ALU.add))
            for j in range(1, 3):
                link(V.scalar_tensor_tensor(out=cv[:, c, :], in0=cx[:, c, j:j + T], scalar=C("conv_w_2", 4 * j + c), in1=cv[:, c, :],
                                            op0=ALU.mult, op1=ALU.add))
        V.tensor_tensor(zb[:, :, :], zb[:, :, :], cv[:, :, :], ALU.mult).then_inc(rec_ready, 1)
        dve.wait_ge(rec_ready, 2)
        attention("b", HD2, 1, K("bound2"))
        wait_emptied(dve, "zg7")
        merged("wa", "wb", 1)
        residual("xp", 1)
        V.nop().then_inc(x_ready, 1)

        stream_norm(3, "ss4", "n4")
        scaled(3)
        V.memset(gpad[:, :, :], -BIG)
        V.memset(keyb[:, :, :], KEY_OUT)
        V.memset(wb[:, :, :], 0.0)
        link(V.memset(etabf, 0.0))
        a0 = ROW["b_rg_2"][0]
        for t in range(TT):
            freed(f"rt{t}", V.tensor_tensor(logit[:, t, :], take(f"rt{t}")[:, 0:36], rowv[:, a0:a0 + 36], ALU.add))
        i4c, i32c = K("iota32")[:, 0:4], K("iota32")
        link(V.tensor_copy(gpad[:, :, 0:4], logit[:, :, 0:4]))
        for t in range(TT):
            link(V.max(out=top8[:, 0, t, :], in_=gpad[:, t, :]))
            link(V.max_index(out=idx8[:, 0, t, :], in_max=top8[:, 0, t, :], in_values=gpad[:, t, :]))
        link(V.tensor_copy(idxf[:, 0, :, :], idx8[:, 0, :, :]))
        for t in range(TT):
            link(V.tensor_scalar(gmask[:, t, :], i4c, idxf[:, 0, t, 0:1], 0.5, ALU.is_equal, ALU.subtract))
            link(V.tensor_scalar(gmask[:, t, :], gmask[:, t, :], 2.0e38, None, ALU.mult))
            link(V.tensor_tensor(emask[:, t, :].rearrange("p (a b) -> p a b", a=4), logit[:, t, 4:36].rearrange("p (a b) -> p a b", a=4),
                                 gmask[:, t, :].unsqueeze(2).to_broadcast([P, 4, 8]), ALU.min))
            link(V.max(out=top8[:, 1, t, :], in_=emask[:, t, :]))
            link(V.max_index(out=idx8[:, 1, t, :], in_max=top8[:, 1, t, :], in_values=emask[:, t, :]))
        link(V.tensor_copy(idxf[:, 1, :, :], idx8[:, 1, :, :]))
        link(V.tensor_tensor(logit[:, :, 0:4], logit[:, :, 0:4], top8[:, 0, :, 0:1].to_broadcast([P, TT, 4]), ALU.subtract))
        V.nop().then_inc(routed_ready, 1)
        link(V.tensor_tensor(gate2v[:, :, 0:1], top8[:, 1, :, 1:2], top8[:, 1, :, 0:1], ALU.subtract))
        V.nop().then_inc(routed_ready, 1)
        dve.wait_ge(route_exp, 2)
        link(V.tensor_reduce(out=gate2v[:, :, 2:3], in_=gexp4[:, :, :], axis=AX.X, op=ALU.add))
        link(V.reciprocal(gate2v[:, :, 3:4], gate2v[:, :, 2:3]))
        link(V.tensor_scalar(gate2v[:, :, 4:5], gate2v[:, :, 1:2], 1.0, None, ALU.add))
        link(V.reciprocal(gate2v[:, :, 5:6], gate2v[:, :, 4:5]))
        link(V.tensor_tensor(gate2v[:, :, 6:7], gate2v[:, :, 5:6], gate2v[:, :, 3:4], ALU.mult))
        link(V.tensor_tensor(gate2v[:, :, 7:8], gate2v[:, :, 6:7], gate2v[:, :, 1:2], ALU.mult))
        for t in range(TT):
            link(V.tensor_scalar(assign[:, t, :], i32c, idxf[:, 1, t, 0:1], None, ALU.is_equal))
            link(V.tensor_scalar(awt[:, t, :], i32c, idxf[:, 1, t, 0:1], gate2v[:, t, 6:7], ALU.is_equal, ALU.mult))
            link(V.tensor_scalar(hot1, i32c, idxf[:, 1, t, 1:2], None, ALU.is_equal))
            link(V.tensor_tensor(assign[:, t, :], assign[:, t, :], hot1, ALU.add))
            link(V.scalar_tensor_tensor(out=awt[:, t, :], in0=hot1, scalar=gate2v[:, t, 7:8], in1=awt[:, t, :], op0=ALU.mult, op1=ALU.add))
        V.nop().then_inc(assign_ready, 1)
        freed("cnt", V.tensor_copy(cntv, take("cnt")[:, 0:32]))
        link(V.memset(extra, 0.0))
        for n in range(1, T // SLOTS):
            link(V.scalar_tensor_tensor(out=extra, in0=cntv, scalar=float(n * SLOTS), in1=extra, op0=ALU.is_gt, op1=ALU.add))
        link(V.tensor_tensor_scan(out=cum, data0=ones[:, 0:32], data1=extra, initial=0.0, op0=ALU.mult, op1=ALU.add))
        link(V.tensor_tensor(start, cum, extra, ALU.subtract))
        freed("pos", V.scalar_tensor_tensor(out=kplus[:, :, :], in0=take("pos")[:, 0:64].rearrange("p (t n) -> p t n", t=TT), scalar=-KEY_OUT,
                                            in1=assign[:, :, :], op0=ALU.add, op1=ALU.mult))
        V.tensor_scalar(keyb[:, :, 0:32], kplus[:, :, :], KEY_OUT, None, ALU.add)
        V.tensor_copy(wb[:, :, 0:32], awt[:, :, :])
        link(V.tensor_copy(etabf[:, 0:32], i32c))
        io = K("iota32")[:, 0:OVER].unsqueeze(2).to_broadcast([P, OVER, NEXP])
        V.tensor_tensor(oh[:, :, :], io, start.unsqueeze(1).to_broadcast([P, OVER, NEXP]), ALU.is_ge)
        link(V.tensor_tensor(oh2[:, :, :], io, cum.unsqueeze(1).to_broadcast([P, OVER, NEXP]), ALU.is_lt))
        link(V.tensor_tensor(oh[:, :, :], oh[:, :, :], oh2[:, :, :], ALU.mult))
        link(V.tensor_reduce(out=oact, in_=oh[:, :, :], axis=AX.X, op=ALU.add))
        link(V.tensor_tensor(oh2[:, :, :], oh[:, :, :], i32c.unsqueeze(1).to_broadcast([P, OVER, NEXP]), ALU.mult))
        link(V.tensor_reduce(out=etabf[:, 32:48], in_=oh2[:, :, :], axis=AX.X, op=ALU.add))
        link(V.tensor_scalar(oshift, K("iota32")[:, 0:OVER], 1.0, float(SLOTS), ALU.add, ALU.mult))
        link(V.tensor_tensor(oshift, oshift, oact, ALU.mult))
        link(V.tensor_scalar(oshift, oshift, -KEY_OUT, None, ALU.add))
        for t in range(TT):
            link(V.scalar_tensor_tensor(out=kplus[:, t, :], in0=start, scalar=float(SLOTS), in1=kplus[:, t, :], op0=ALU.mult, op1=ALU.add))
            link(V.tensor_tensor(oh2[:, :, :], oh[:, :, :], kplus[:, t, :].unsqueeze(1).to_broadcast([P, OVER, NEXP]), ALU.mult))
            link(V.tensor_reduce(out=keyb[:, t, 32:48], in_=oh2[:, :, :], axis=AX.X, op=ALU.add))
            link(V.tensor_tensor(keyb[:, t, 32:48], keyb[:, t, 32:48], oshift, ALU.subtract))
            link(V.tensor_tensor(oh2[:, :, :], oh[:, :, :], awt[:, t, :].unsqueeze(1).to_broadcast([P, OVER, NEXP]), ALU.mult))
            link(V.tensor_reduce(out=wb[:, t, 32:48], in_=oh2[:, :, :], axis=AX.X, op=ALU.add))
        link(V.tensor_scalar(etabf[:, 50:51], cum[:, 31:32], float(NEXP + 1), None, ALU.add))
        link(V.tensor_copy(etab[:, :], etabf))
        link(V.tensor_single_scalar(npair_sb, npair_sb, 1, ALU.logical_shift_right))

        slot4 = K("slot4")

        def pick_of(par, b):
            for t in range(TT):
                ins = V.tensor_scalar(pick[:, par, t, :], slot4[:, 0:SLOTS], keyb[:, t, bass.ds(b, 1)], None, ALU.is_equal)
            ins.then_inc(pick_ready, 1)

        link(V.memset(y4s[:, 1, :], 0.0))
        link(V.memset(placeT[:, 1, :], 0.0))
        V.nop().then_inc(table_ready, 1)
        for s in (y0_out, y1_out, placeT_out, hid_ready, m_pwt):
            V.nop().then_inc(s, 1)
        pick_of(0, 0)
        pick_of(1, 1)
        dve.wait_ge(m_x4, 1)
        wait_emptied(dve, "hu3")
        V.tensor_copy(x4s, ps[5][:, :]).then_inc(x4_out, 1)
        npair = dve.value_load(npair_sb[0:1, :], min_val=NEXP // 2, max_val=(NEXP + OVER) // 2)
        with dve.Fori(0, npair) as i:
            for par in range(2):
                n1 = i * 2 + (par + 1)
                dve.wait_ge(m_pwt, n1)
                for t in range(TT):
                    ins = V.tensor_scalar(place[:, t, :], slot4, keyb[:, t, bass.ds(i * 2 + par, 1)], wb[:, t, bass.ds(i * 2 + par, 1)],
                                          ALU.is_equal, ALU.mult)
                ins.then_inc(place_ready, 1)
                dve.wait_ge(m_x4, n1 + 1)
                V.tensor_copy(x4s, ps[5][:, :]).then_inc(x4_out, 1)
                dve.wait_ge(silu_out, n1)
                V.tensor_tensor(hts[:, :, :], sil[:, :, :], ps[6][:, 0:T].rearrange("p (c a s) -> p c a s", c=4, a=2)[:, :, 1, :], ALU.mult)\
                    .then_inc(hid_ready, 1)
                pick_of(par, i * 2 + (par + 2))
                dve.wait_ge(m_w2, n1 * 2)
                V.tensor_copy(y4s[:, par, 512:D], ps[5][:, :]).then_inc(y1_out, 1)
        dve.wait_ge(m_comb, npair * 2 + 2)
        for c in range(DC):
            ins = V.scalar_tensor_tensor(out=outT[:, c, :], in0=ps[c // 2][:, (c % 2) * T:(c % 2 + 1) * T], scalar=mod[:, 1, 40 + c:41 + c],
                                         in1=xT[:, c, :], op0=ALU.mult, op1=ALU.add)
        ins.then_inc(x_ready, 1)


def kernel(**inputs):
    import concourse.bacc as bacc
    from concourse.bass_utils import run_bass_kernel_spmd

    a = {k: np.asarray(v) for k, v in inputs.items()}

    def per_partition(v):
        return v.reshape(-1, P).T

    COL, NCOL = columns_layout()
    columns = np.zeros((P, NCOL), np.float32)
    for name, (lo, hi) in COL.items():
        v = a[name].reshape(-1)
        columns[:, lo:hi] = per_partition(v)
    ROW, NROWV = rows_layout()
    rowv = np.zeros((NROWV,), np.float32)
    for name, (lo, hi) in ROW.items():
        rowv[lo:hi] = a[name].reshape(-1)

    arrays = {
        "xT": a["x"][0].T.reshape(DC, P, T).transpose(1, 0, 2),
        "columns": columns,
        "rows": rowv,
        "constants": constants()[1],
        "pos": a["positions"][0].reshape(TT, P).T,
        "keysT": a["sub_keys"][0].transpose(3, 0, 1, 2).reshape(P, 2 * PH, NKEY),
        "w_route": np.concatenate([a["w_rg_2"][0], a["w_re_2"][0]], axis=1),
    }
    for name in ("w_ada", "w_in", "w_uq", "w_ukv", "w_o_attn", "w_rg", "w_ig", "w_o_lru", "w_out", "w_query", "expert_u", "expert_v",
                 "w_ada_2", "w_in_2", "w_pa_2", "w_pb_2", "w_o_2", "w1_2", "w3_2", "w2_2"):
        arrays[name] = a[name][0]
    arrays = {k: np.ascontiguousarray(v) for k, v in arrays.items()}

    nc = bacc.Bacc("TRN2", target_bir_lowering=False, num_devices=1)
    g = {k: nc.dram_tensor(f"in_{k}", v.shape, mybir.dt.from_np(v.dtype), kind="ExternalInput").ap() for k, v in arrays.items()}
    out = nc.dram_tensor("out_xT", (P, DC, T), F32, kind="ExternalOutput").ap()
    build(nc, g, out)
    r = run_bass_kernel_spmd(nc, [{f"in_{k}": v for k, v in arrays.items()}], core_ids=[0])
    got = np.asarray(r.results[0]["out_xT"])
    return np.ascontiguousarray(got.transpose(1, 0, 2).reshape(D, T).T)[None]
```
